# Optimizing a Trainium2 kernel written in Bass

```python
import jax, jax.numpy as jnp
from jax import lax
import numpy as np
import math
import jax
import jax.numpy as jnp

D_MODEL = 2048
BATCH = 1
SEQ = 256
DEPTH = 2

HEAD_DIM = 128
ATTN_WIDTH = D_MODEL // 2
N_Q_HEADS = ATTN_WIDTH // HEAD_DIM
N_KV_HEADS = max(1, N_Q_HEADS // 4)
GQA_GROUP = N_Q_HEADS // N_KV_HEADS
KV_WIDTH = N_KV_HEADS * HEAD_DIM
WINDOW = 128
BLOCK = 128
GMLP_WIDTH = D_MODEL - ATTN_WIDTH
GMLP_HEAD_DIM = 128
N_GMLP_HEADS = GMLP_WIDTH // GMLP_HEAD_DIM
CHUNK = 128
IN_WIDTH = ATTN_WIDTH + 2 * KV_WIDTH + 2 * GMLP_WIDTH
D_FF = 5632
CONV_WIDTH = 3
ROPE_THETA = 10000.0
EPS = 1e-6
MASK_VALUE = -1e30


def rms_norm(x, g):
    xf = x.astype(jnp.float32)
    y = xf * lax.rsqrt(jnp.mean(xf * xf, axis=-1, keepdims=True) + EPS)
    return (y * g.astype(jnp.float32)).astype(x.dtype)

def layer_norm(x, g, b):
    xf = x.astype(jnp.float32)
    mu = jnp.mean(xf, axis=-1, keepdims=True)
    xc = xf - mu
    y = xc * lax.rsqrt(jnp.mean(xc * xc, axis=-1, keepdims=True) + EPS)
    return (y * g.astype(jnp.float32) + b.astype(jnp.float32)).astype(x.dtype)

def rope_tables(seq):
    inv_freq = ROPE_THETA ** (-jnp.arange(0, HEAD_DIM, 2, dtype=jnp.float32) / HEAD_DIM)
    ang = jnp.arange(seq, dtype=jnp.float32)[:, None] * inv_freq[None, :]
    return jnp.cos(ang), jnp.sin(ang)

def apply_rope(x, cos, sin):
    xf = x.astype(jnp.float32)
    x1, x2 = jnp.split(xf, 2, axis=-1)
    c = cos[None, :, None, :]
    s = sin[None, :, None, :]
    return jnp.concatenate([x1 * c - x2 * s, x2 * c + x1 * s], axis=-1).astype(x.dtype)

def banded_window_attention(q, k, v, sink):
    B, S, _, D = q.shape
    nb = S // BLOCK
    qb = q.reshape(B, nb, BLOCK, N_KV_HEADS, GQA_GROUP, D)

    def band(t):
        tp = jnp.pad(t, ((0, 0), (BLOCK, BLOCK), (0, 0), (0, 0)))
        tp = tp.reshape(B, nb + 2, BLOCK, N_KV_HEADS, D)
        return jnp.concatenate([tp[:, :-2], tp[:, 1:-1], tp[:, 2:]], axis=2)

    kb, vb = band(k), band(v)
    s = jnp.einsum('bnqhgd,bnkhd->bnhgqk', qb, kb).astype(jnp.float32) * (D ** -0.5)
    blk = jnp.arange(nb)[:, None, None]
    q_pos = blk * BLOCK + jnp.arange(BLOCK)[None, :, None]
    k_pos = blk * BLOCK - BLOCK + jnp.arange(3 * BLOCK)[None, None, :]
    valid = (jnp.abs(k_pos - q_pos) <= WINDOW) & (k_pos >= 0) & (k_pos < S)
    s = jnp.where(valid[None, :, None, None], s, MASK_VALUE)
    sk = sink.astype(jnp.float32).reshape(N_KV_HEADS, GQA_GROUP)[None, None, :, :, None, None]
    m = jnp.maximum(jnp.max(s, axis=-1, keepdims=True), sk)
    p = jnp.exp(s - m)
    probs = p / (jnp.sum(p, axis=-1, keepdims=True) + jnp.exp(sk - m))
    out = jnp.einsum('bnhgqk,bnkhd->bnqhgd', probs.astype(v.dtype), vb)
    return out.reshape(B, S, N_Q_HEADS * D)

def chunked_spatial_gating(u, v, ln_g, ln_b, w_s, b_s):
    B, S, _ = u.shape
    nc = S // CHUNK
    vn = layer_norm(v, ln_g, ln_b).reshape(B, nc, CHUNK, N_GMLP_HEADS, GMLP_HEAD_DIM)
    f = jnp.einsum('hpq,bcqhd->bcphd', w_s, vn) + b_s.T[None, None, :, :, None]
    return u * f.reshape(B, S, GMLP_WIDTH)

def depthwise_conv_centred(h, w, b):
    S = h.shape[1]
    half = CONV_WIDTH // 2
    hp = jnp.pad(h, ((0, 0), (half, half), (0, 0)))
    out = b
    for t in range(CONV_WIDTH):
        out = out + hp[:, t:t + S] * w[t]
    return out

def conv_gated_ffn(h, w_up, conv_w, conv_b, w_down):
    a = depthwise_conv_centred(h @ w_up, conv_w, conv_b)
    g, u = jnp.split(a, 2, axis=-1)
    return (jax.nn.silu(g) * u) @ w_down

def first_inputs(seed: int = 0) -> dict:
    key = jax.random.key(seed)
    ks = jax.random.split(key, 20)
    f32 = jnp.float32
    nrm = lambda k, shape, scale: jax.random.normal(k, shape, f32) * scale
    res_scale = (2.0 * DEPTH) ** -0.5
    return {
        "x": jax.random.normal(ks[0], (BATCH, SEQ, D_MODEL), f32),
        "norm1_g": 1.0 + nrm(ks[1], (DEPTH, D_MODEL), 0.02),
        "w_in": nrm(ks[2], (DEPTH, D_MODEL, IN_WIDTH), D_MODEL ** -0.5),
        "q_norm_g": 1.0 + nrm(ks[3], (DEPTH, HEAD_DIM), 0.02),
        "k_norm_g": 1.0 + nrm(ks[4], (DEPTH, HEAD_DIM), 0.02),
        "sink": nrm(ks[5], (DEPTH, N_Q_HEADS), 0.5),
        "sgu_ln_g": 1.0 + nrm(ks[6], (DEPTH, GMLP_WIDTH), 0.02),
        "sgu_ln_b": nrm(ks[7], (DEPTH, GMLP_WIDTH), 0.02),
        "w_s": nrm(ks[8], (DEPTH, N_GMLP_HEADS, CHUNK, CHUNK), 0.5 * CHUNK ** -0.5),
        "b_s": 1.0 + nrm(ks[9], (DEPTH, N_GMLP_HEADS, CHUNK), 0.02),
        "attn_out_g": 1.0 + nrm(ks[10], (DEPTH, ATTN_WIDTH), 0.02),
        "sgu_out_g": 1.0 + nrm(ks[11], (DEPTH, GMLP_WIDTH), 0.02),
        "w_o": nrm(ks[12], (DEPTH, D_MODEL, D_MODEL), D_MODEL ** -0.5 * res_scale),
        "norm2_g": 1.0 + nrm(ks[13], (DEPTH, D_MODEL), 0.02),
        "w_up": nrm(ks[14], (DEPTH, D_MODEL, 2 * D_FF), D_MODEL ** -0.5),
        "conv_w": nrm(ks[15], (DEPTH, CONV_WIDTH, 2 * D_FF), CONV_WIDTH ** -0.5),
        "conv_b": nrm(ks[16], (DEPTH, 2 * D_FF), 0.01),
        "w_down": nrm(ks[17], (DEPTH, D_FF, D_MODEL), D_FF ** -0.5 * res_scale),
    }

def first_block(x, norm1_g, w_in, q_norm_g, k_norm_g, sink, sgu_ln_g, sgu_ln_b, w_s, b_s,
              attn_out_g, sgu_out_g, w_o, norm2_g, w_up, conv_w, conv_b, w_down):
    B, S, _ = x.shape
    cos, sin = rope_tables(S)
    splits = [ATTN_WIDTH, ATTN_WIDTH + KV_WIDTH, ATTN_WIDTH + 2 * KV_WIDTH,
              ATTN_WIDTH + 2 * KV_WIDTH + GMLP_WIDTH]
    for l in range(DEPTH):
        h = rms_norm(x, norm1_g[l])
        q, k, v, gu, gv = jnp.split(h @ w_in[l], splits, axis=-1)
        q = apply_rope(rms_norm(q.reshape(B, S, N_Q_HEADS, HEAD_DIM), q_norm_g[l]), cos, sin)
        k = apply_rope(rms_norm(k.reshape(B, S, N_KV_HEADS, HEAD_DIM), k_norm_g[l]), cos, sin)
        v = v.reshape(B, S, N_KV_HEADS, HEAD_DIM)
        attn = banded_window_attention(q, k, v, sink[l])
        sgu = chunked_spatial_gating(jax.nn.gelu(gu), jax.nn.gelu(gv),
                                     sgu_ln_g[l], sgu_ln_b[l], w_s[l], b_s[l])
        mixed = jnp.concatenate([rms_norm(attn, attn_out_g[l]), rms_norm(sgu, sgu_out_g[l])], axis=-1)
        x = x + mixed @ w_o[l]
        x = x + conv_gated_ffn(rms_norm(x, norm2_g[l]), w_up[l], conv_w[l], conv_b[l], w_down[l])
    return x


DEPTH_2 = 1

CTX_LEN = 256
GRID_W = 64
N_MOD = 6
D_MIX = D_MODEL
HY_W = D_MIX // 2
HY_GROUPS = 8
HY_ORDER = 2
HY_PROJ = (HY_ORDER + 1) * HY_W
HY_CONV = 3
HY_POS_EMB = 33
HY_FILT_H = 64
HY_TARGET = 1e-2
HY_FAST = 0.3
HY_SLOW = 1.5
SSD_W = D_MIX - HY_W
SSD_HEADDIM = 64
SSD_HEADS = SSD_W // SSD_HEADDIM
SSD_GROUPS = 2
SSD_HPG = SSD_HEADS // SSD_GROUPS
SSD_STATE = 128
SSD_CONV = 3
SSD_CHUNK = 128
SSD_XBC = SSD_W + 2 * SSD_GROUPS * SSD_STATE
SSD_DT = 2 * SSD_HEADS
PROJ_W = HY_PROJ + SSD_XBC + SSD_DT + SSD_W
D_FF_2 = 4 * D_MODEL


def rmsnorm(x, w):
    xf = x.astype(jnp.float32)
    y = xf * lax.rsqrt(jnp.mean(xf * xf, axis=-1, keepdims=True) + EPS)
    return (y * w).astype(x.dtype)

def centred_dwconv(u, w, bias, grid):
    b, L, C = u.shape
    if grid is not None:
        u = u.reshape(b, grid[0], grid[1], C)
    K = w.shape[0]
    pad = K // 2
    T = u.shape[-2]
    up = jnp.pad(u, [(0, 0)] * (u.ndim - 2) + [(pad, pad), (0, 0)])
    y = bias + w[0] * up[..., 0:T, :]
    for k in range(1, K):
        y = y + w[k] * up[..., k:k + T, :]
    return y.reshape(b, L, C)

def hyena_kernel_fft(L, fw1, fb1, freq, fw2, fb2, fw3):
    f32 = jnp.float32
    t = jnp.linspace(0.0, 1.0, L, dtype=f32)[:, None]
    bands = (HY_POS_EMB - 1) // 2
    w = 2.0 * math.pi * jnp.arange(L, dtype=f32)[:, None] / L
    f = jnp.linspace(1e-4, bands - 1, bands, dtype=f32)[None, :]
    feats = jnp.concatenate([t, jnp.cos(f * w), -jnp.sin(f * w)], axis=-1)
    hdn = jnp.sin(freq * (feats @ fw1 + fb1))
    hdn = jnp.sin(freq * (hdn @ fw2 + fb2))
    h = (hdn @ fw3).astype(f32).reshape(L, HY_ORDER, 2, HY_W)
    deltas = jnp.linspace(math.log(HY_TARGET) / HY_SLOW, math.log(HY_TARGET) / HY_FAST, HY_W, dtype=f32)
    h = h * jnp.exp(-t[:, :, None, None] * jnp.abs(deltas))
    k = jnp.concatenate([h[:, :, 0], jnp.zeros((1, HY_ORDER, HY_W), f32), h[:0:-1, :, 1]], axis=0)
    k = k / (jnp.sum(jnp.abs(k), axis=0, keepdims=True) + EPS)
    return jnp.fft.rfft(k, axis=0)

def fft_conv(z, kf):
    L = z.shape[1]
    zf = jnp.fft.rfft(z, n=2 * L, axis=1)
    return jnp.fft.irfft(zf * kf[None], n=2 * L, axis=1)[:, :L]

def segsum(a):
    T = a.shape[-1]
    cs = jnp.cumsum(a, axis=-1)
    diff = cs[..., :, None] - cs[..., None, :]
    mask = jnp.tril(jnp.ones((T, T), dtype=bool))
    return jnp.where(mask, diff, -jnp.inf)

def ssd_scan(xdt, da, bm, cm, init, want_y):
    b, l, g, r, p = xdt.shape
    nc = l // SSD_CHUNK
    xdt = xdt.reshape(b, nc, SSD_CHUNK, g, r, p)
    bc = bm.reshape(b, nc, SSD_CHUNK, g, -1)
    a = da.reshape(b, nc, SSD_CHUNK, g, r).transpose(0, 3, 4, 1, 2)
    a_cs = jnp.cumsum(a, axis=-1)
    decay_to_end = jnp.exp(a_cs[..., -1:] - a_cs)
    states = jnp.einsum('bcsgn,bgrcs,bcsgrp->bcgrpn', bc, decay_to_end, xdt)
    chunk_a = jnp.pad(a_cs[..., -1], ((0, 0), (0, 0), (0, 0), (1, 0)))
    states_all = jnp.concatenate([init[:, None], states], axis=1)
    carried = jnp.einsum('bgrzc,bcgrpn->bzgrpn', jnp.exp(segsum(chunk_a)), states_all)
    final = carried[:, -1]
    if not want_y:
        return final
    cc = cm.reshape(b, nc, SSD_CHUNK, g, -1)
    cb = jnp.einsum('bclgn,bcsgn->bgcls', cc, bc)
    y_diag = jnp.einsum('bgcls,bgrcls,bcsgrp->bclgrp', cb, jnp.exp(segsum(a)), xdt)
    y_off = jnp.einsum('bclgn,bcgrpn,bgrcl->bclgrp', cc, carried[:, :-1], jnp.exp(a_cs))
    y = (y_diag + y_off).reshape(b, l, g, r, p)
    return y, final

def ssd_branch(h, init_f, init_b, grid, lp, want_y):
    b, L, _ = h.shape
    f32 = jnp.float32
    w_in = lp['w_in']
    o0 = HY_PROJ
    o1 = o0 + SSD_XBC
    o2 = o1 + SSD_DT
    xbc = jax.nn.silu(centred_dwconv(h @ w_in[:, o0:o1], lp['ssd_conv_w'], lp['ssd_conv_b'], grid)).astype(f32)
    gn = SSD_GROUPS * SSD_STATE
    xs = xbc[..., :SSD_W].reshape(b, L, SSD_GROUPS, SSD_HPG, SSD_HEADDIM)
    bm = xbc[..., SSD_W:SSD_W + gn].reshape(b, L, SSD_GROUPS, SSD_STATE)
    cm = xbc[..., SSD_W + gn:].reshape(b, L, SSD_GROUPS, SSD_STATE)
    dt = jax.nn.softplus((h @ w_in[:, o1:o2]).astype(f32).reshape(b, L, 2, SSD_HEADS) + lp['dt_bias'])
    dt = dt.reshape(b, L, 2, SSD_GROUPS, SSD_HPG)
    a = (-jnp.exp(lp['a_log'].astype(f32))).reshape(2, SSD_GROUPS, SSD_HPG)

    def run(d, init, flip):
        dt_d = dt[:, :, d]
        seqs = (xs * dt_d[..., None], dt_d * a[d], bm, cm)
        if flip:
            seqs = tuple(s[:, ::-1] for s in seqs)
        return ssd_scan(seqs[0], seqs[1], seqs[2], seqs[3], init, want_y)

    if not want_y:
        return run(0, init_f, False), run(1, init_b, True)
    y_f, s_f = run(0, init_f, False)
    y_b, s_b = run(1, init_b, True)
    y = y_f + y_b[:, ::-1] + lp['ssd_d'].reshape(SSD_GROUPS, SSD_HPG)[..., None] * xs
    zg = jax.nn.silu((h @ w_in[:, o2:]).astype(f32))
    y = (y.reshape(b, L, SSD_W) * zg).reshape(b, L, SSD_GROUPS, SSD_W // SSD_GROUPS)
    y = rmsnorm(y, lp['ssd_norm_w'].reshape(SSD_GROUPS, -1)).reshape(b, L, SSD_W)
    return y.astype(h.dtype), s_f, s_b

def token_mixer(h, init_f, init_b, grid, lp):
    b, L, _ = h.shape
    u = centred_dwconv(h @ lp['w_in'][:, :HY_PROJ], lp['hy_conv_w'], lp['hy_conv_b'], grid).astype(jnp.float32)
    v, *gates = jnp.split(u, HY_ORDER + 1, axis=-1)
    kf = hyena_kernel_fft(L, lp['filt_w1'], lp['filt_b1'], lp['filt_freq'], lp['filt_w2'], lp['filt_b2'], lp['filt_w3'])
    z = v
    for o, gate in enumerate(gates):
        z = gate * (fft_conv(z, kf[:, o]) + z * lp['hy_bias'][o])
    y_hy = rmsnorm(z.reshape(b, L, HY_GROUPS, HY_W // HY_GROUPS), lp['hy_norm_w'].reshape(HY_GROUPS, -1))
    y_hy = y_hy.reshape(b, L, HY_W).astype(h.dtype)
    y_ssd, s_f, s_b = ssd_branch(h, init_f, init_b, grid, lp, True)
    out = jnp.concatenate([y_hy, y_ssd], axis=-1) @ lp['w_out']
    return out, s_f, s_b

def sqrelu_mlp(h, w1, w2):
    return jnp.square(jax.nn.relu(h @ w1)) @ w2

def second_inputs(seed: int = 0) -> dict:
    key = jax.random.key(seed)
    ks = jax.random.split(key, 32)

    def nrm(k, shape, scale):
        return scale * jax.random.normal(k, shape, jnp.float32)

    D = D_MODEL
    dt0 = jnp.exp(jax.random.uniform(ks[20], (DEPTH_2, 2, SSD_HEADS), jnp.float32, math.log(1e-3), math.log(1e-1)))
    return {
        'x': nrm(ks[0], (BATCH, SEQ, D), 1.0),
        'c': nrm(ks[1], (BATCH, D), 1.0),
        'ctx': nrm(ks[2], (BATCH, CTX_LEN, D), 1.0),
        'c_ctx': nrm(ks[3], (D,), 1.0),
        'w_ada': nrm(ks[4], (DEPTH_2, D, N_MOD * D), 0.5 * D ** -0.5),
        'b_ada': nrm(ks[5], (DEPTH_2, N_MOD * D), 0.02),
        'norm1_w': 1.0 + nrm(ks[6], (DEPTH_2, D), 0.05),
        'w_in': nrm(ks[7], (DEPTH_2, D, PROJ_W), D ** -0.5),
        'hy_conv_w': nrm(ks[8], (DEPTH_2, HY_CONV, HY_PROJ), HY_CONV ** -0.5),
        'hy_conv_b': nrm(ks[9], (DEPTH_2, HY_PROJ), 0.02),
        'filt_w1': nrm(ks[10], (DEPTH_2, HY_POS_EMB, HY_FILT_H), HY_POS_EMB ** -0.5),
        'filt_b1': nrm(ks[11], (DEPTH_2, HY_FILT_H), 0.1),
        'filt_freq': 1.0 + nrm(ks[12], (DEPTH_2, HY_FILT_H), 0.1),
        'filt_w2': nrm(ks[13], (DEPTH_2, HY_FILT_H, HY_FILT_H), HY_FILT_H ** -0.5),
        'filt_b2': nrm(ks[14], (DEPTH_2, HY_FILT_H), 0.1),
        'filt_w3': nrm(ks[15], (DEPTH_2, HY_FILT_H, HY_ORDER * 2 * HY_W), HY_FILT_H ** -0.5),
        'hy_bias': nrm(ks[16], (DEPTH_2, HY_ORDER, HY_W), 0.1),
        'hy_norm_w': 1.0 + nrm(ks[17], (DEPTH_2, HY_W), 0.05),
        'ssd_conv_w': nrm(ks[18], (DEPTH_2, SSD_CONV, SSD_XBC), SSD_CONV ** -0.5),
        'ssd_conv_b': nrm(ks[19], (DEPTH_2, SSD_XBC), 0.02),
        'dt_bias': dt0 + jnp.log(-jnp.expm1(-dt0)),
        'a_log': jnp.log(jax.random.uniform(ks[21], (DEPTH_2, 2, SSD_HEADS), jnp.float32, 1.0, 16.0)),
        'ssd_d': 1.0 + nrm(ks[22], (DEPTH_2, SSD_HEADS), 0.05),
        'ssd_norm_w': 1.0 + nrm(ks[23], (DEPTH_2, SSD_W), 0.05),
        'w_out': nrm(ks[24], (DEPTH_2, D_MIX, D), D_MIX ** -0.5),
        'norm2_w': 1.0 + nrm(ks[25], (DEPTH_2, D), 0.05),
        'w_mlp1': nrm(ks[26], (DEPTH_2, D, D_FF_2), D ** -0.5),
        'w_mlp2': nrm(ks[27], (DEPTH_2, D_FF_2, D), D_FF_2 ** -0.5),
        'final_norm_w': 1.0 + nrm(ks[28], (D,), 0.05),
    }

def second_block(x, c, ctx, c_ctx, w_ada, b_ada, norm1_w, w_in, hy_conv_w, hy_conv_b, filt_w1, filt_b1,
              filt_freq, filt_w2, filt_b2, filt_w3, hy_bias, hy_norm_w, ssd_conv_w, ssd_conv_b, dt_bias,
              a_log, ssd_d, ssd_norm_w, w_out, norm2_w, w_mlp1, w_mlp2, final_norm_w):
    rows = x.shape[1] // GRID_W
    grid = (rows, GRID_W)
    zero_state = jnp.zeros((x.shape[0], SSD_GROUPS, SSD_HPG, SSD_HEADDIM, SSD_STATE), jnp.float32)
    h_ctx = ctx
    for i in range(DEPTH_2):
        lp = dict(w_in=w_in[i], hy_conv_w=hy_conv_w[i], hy_conv_b=hy_conv_b[i], filt_w1=filt_w1[i],
                  filt_b1=filt_b1[i], filt_freq=filt_freq[i], filt_w2=filt_w2[i], filt_b2=filt_b2[i],
                  filt_w3=filt_w3[i], hy_bias=hy_bias[i], hy_norm_w=hy_norm_w[i], ssd_conv_w=ssd_conv_w[i],
                  ssd_conv_b=ssd_conv_b[i], dt_bias=dt_bias[i], a_log=a_log[i], ssd_d=ssd_d[i],
                  ssd_norm_w=ssd_norm_w[i], w_out=w_out[i])
        mod = (jax.nn.silu(c) @ w_ada[i] + b_ada[i])[:, None, :]
        mod_c = jax.nn.silu(c_ctx) @ w_ada[i] + b_ada[i]
        sh1, sc1, g1, sh2, sc2, g2 = jnp.split(mod, N_MOD, axis=-1)
        csh1, csc1, cg1, csh2, csc2, cg2 = jnp.split(mod_c, N_MOD, axis=-1)
        hc = rmsnorm(h_ctx, norm1_w[i]) * (1.0 + csc1) + csh1
        if i < DEPTH_2 - 1:
            out_c, s_f, s_b = token_mixer(hc, zero_state, zero_state, None, lp)
            h_ctx = h_ctx + cg1 * out_c
            hc2 = rmsnorm(h_ctx, norm2_w[i]) * (1.0 + csc2) + csh2
            h_ctx = h_ctx + cg2 * sqrelu_mlp(hc2, w_mlp1[i], w_mlp2[i])
        else:
            s_f, s_b = ssd_branch(hc, zero_state, zero_state, None, lp, False)
        hl = rmsnorm(x, norm1_w[i]) * (1.0 + sc1) + sh1
        out_l, _, _ = token_mixer(hl, s_f, s_b, grid, lp)
        x = x + g1 * out_l
        hl2 = rmsnorm(x, norm2_w[i]) * (1.0 + sc2) + sh2
        x = x + g2 * sqrelu_mlp(hl2, w_mlp1[i], w_mlp2[i])
    return rmsnorm(x, final_norm_w)


def setup_inputs(seed=0):
    out = dict(first_inputs(seed))
    for name, value in second_inputs(seed + 1).items():
        if name != "x":
            out[name + "_2"] = value
    return out


def reference(
    x, norm1_g, w_in, q_norm_g, k_norm_g, sink, sgu_ln_g, sgu_ln_b, w_s, b_s, attn_out_g,
    sgu_out_g, w_o, norm2_g, w_up, conv_w, conv_b, w_down, c_2, ctx_2, c_ctx_2, w_ada_2,
    b_ada_2, norm1_w_2, w_in_2, hy_conv_w_2, hy_conv_b_2, filt_w1_2, filt_b1_2, filt_freq_2,
    filt_w2_2, filt_b2_2, filt_w3_2, hy_bias_2, hy_norm_w_2, ssd_conv_w_2, ssd_conv_b_2,
    dt_bias_2, a_log_2, ssd_d_2, ssd_norm_w_2, w_out_2, norm2_w_2, w_mlp1_2, w_mlp2_2,
    final_norm_w_2,
):
    x = first_block(
        x, norm1_g, w_in, q_norm_g, k_norm_g, sink, sgu_ln_g, sgu_ln_b, w_s, b_s, attn_out_g,
        sgu_out_g, w_o, norm2_g, w_up, conv_w, conv_b, w_down,
    )
    return second_block(
        x, c_2, ctx_2, c_ctx_2, w_ada_2, b_ada_2, norm1_w_2, w_in_2, hy_conv_w_2, hy_conv_b_2,
        filt_w1_2, filt_b1_2, filt_freq_2, filt_w2_2, filt_b2_2, filt_w3_2, hy_bias_2,
        hy_norm_w_2, ssd_conv_w_2, ssd_conv_b_2, dt_bias_2, a_log_2, ssd_d_2, ssd_norm_w_2,
        w_out_2, norm2_w_2, w_mlp1_2, w_mlp2_2, final_norm_w_2,
    )


_drawn_inputs = setup_inputs


def setup_inputs(seed=0):
    import zlib

    import numpy as np

    out = dict(_drawn_inputs(seed))
    spreads = {}
    factors = {'norm1_g': 3.058,
     'q_norm_g': 8.0,
     'k_norm_g': 8.0,
     'sink': 8.0,
     'sgu_ln_g': 8.0,
     'sgu_ln_b': 8.0,
     'b_s': 7.067,
     'attn_out_g': 5.664,
     'sgu_out_g': 5.943,
     'norm2_g': 5.311,
     'conv_b': 8.0,
     'ctx_2': 6.403,
     'c_ctx_2': 8.0,
     'norm1_w_2': 11.172,
     'hy_conv_b_2': 37.171,
     'filt_freq_2': 2.672,
     'hy_norm_w_2': 56.856,
     'ssd_conv_b_2': 64.0,
     'ssd_d_2': 64.0,
     'ssd_norm_w_2': 56.0,
     'norm2_w_2': 11.215}
    for name, (base, spread) in spreads.items():
        noise = np.random.default_rng([zlib.crc32(name.encode()), seed]).standard_normal(out[name].shape)
        drawn = base * np.exp(spread * noise) if base else spread * noise
        out[name] = jnp.asarray(drawn.astype(out[name].dtype))
    for name, factor in factors.items():
        out[name] = (out[name] * factor).astype(out[name].dtype)
    return out
```

```python
import math

import numpy as np

D, TOK, TT, P = 2048, 256, 2, 128
KT = D // P
CH = 512
NS = 4
HD, NQ, NKV = 128, 8, 2
DFF = 5632
FT = DFF // P
NPAIR = DFF // CH
EPS = 1e-6
HYW = SSW = 1024
HY_EMB, HY_HID = 33, 64
NH, PH = 16, 64
SEG = 64
DFF2 = 8192


def shape_constants():
    f32 = np.float32
    c = {}
    c["ident"] = np.eye(P, dtype=f32)
    pos = np.arange(TOK)
    inv_freq = (f32(10000.0) ** (-np.arange(0, HD, 2, dtype=f32) / f32(HD))).astype(f32)
    ang = pos.astype(f32)[:, None] * inv_freq[None, :]
    cos, sin = np.cos(ang).astype(f32), np.sin(ang).astype(f32)
    c["cos"] = cos.reshape(TT, P, 64).transpose(1, 0, 2).copy()
    c["sin"] = np.stack([-sin, sin], 1).reshape(TT, P, 2, 64).transpose(1, 0, 2, 3).copy()
    far = np.abs(pos[:, None] - pos[None, :]) > 128
    c["band"] = np.where(far, f32(-1e30), f32(0)).reshape(TT, P, TOK).transpose(1, 0, 2).astype(f32).copy()
    i = np.arange(P)
    k, q = i[:, None], i[None, :]
    c["masks"] = np.stack([k <= q, k > q, k + q >= 0, k < q, k >= q], 1).astype(f32)
    t = np.linspace(0.0, 1.0, TOK, dtype=f32)[:, None]
    bands = (HY_EMB - 1) // 2
    w = (2.0 * math.pi * pos.astype(f32)[:, None] / f32(TOK)).astype(f32)
    f = np.linspace(1e-4, bands - 1, bands, dtype=f32)[None, :]
    c["feats"] = np.concatenate([t, np.cos(f * w), -np.sin(f * w)], 1).T.astype(f32).copy()
    deltas = np.linspace(math.log(1e-2) / 1.5, math.log(1e-2) / 0.3, HYW, dtype=f32)
    c["decay"] = np.exp(-t * np.abs(deltas)).astype(f32).reshape(TT, P, HYW).transpose(1, 0, 2).copy()
    c["not_first"] = (i > 0).astype(f32)[:, None].copy()
    ang = 2 * np.pi * ((2 * pos[None, :] + 1) * pos[:, None] % (4 * TOK)) / (4 * TOK)
    for name, m in (("dft", [np.cos(ang), np.sin(ang)]), ("idft", [np.cos(ang).T / TOK, np.sin(ang).T / TOK])):
        c[name] = np.stack([v.astype(f32).reshape(TT, P, TOK).transpose(1, 0, 2) for v in m], 1).copy()
    return c


def program(nc, t, out):
    import concourse.bass as bass
    from concourse import mybir

    F32, F32R = mybir.dt.float32, mybir.dt.float32r
    ALU, ACT = mybir.AluOpType, mybir.ActivationFunctionType
    X_AXIS = mybir.AxisListType.X
    ds = bass.ds

    base = [(nc.sbuf_base + 31) // 32 * 32]

    def sb(name, shape, dtype=F32, at=None):
        size = 4 * int(np.prod(shape[1:]))
        if at is None:
            at = base[0]
            base[0] = at + (size + 31) // 32 * 32
        return nc.alloc_sbuf_tensor_at(name, shape, dtype, offset=at), at

    def sbt(name, shape, dtype=F32, at=None):
        return sb(name, shape, dtype, at)[0]

    x_sb = sbt("x_sb", [P, TT, D])
    raw, lo, hi, at_raw, at_hi = [], [], [], [], []
    for s in range(NS):
        r, at = sb(f"w_raw{s}", [P, 4, CH])
        raw.append(r)
        at_raw.append(at)
        lo.append(sbt(f"w_lo{s}", [P, 4, CH], F32R, at))
        r, at = sb(f"w_hi{s}", [P, 4, CH], F32R)
        hi.append(r)
        at_hi.append(at)
    ident = sbt("ident_sb", [P, P])
    cos, at_cos = sb("cos_sb", [P, TT, 64])
    sin = sbt("sin_sb", [P, TT, 2, 64])
    band, at_band = sb("band_sb", [P, TT, TOK])
    one, zero = sbt("one", [P, 1]), sbt("zero", [P, 1])
    table, at_table = sb("table", [P, 408])
    staged = sbt("staged", [P, 5, P])
    mod = sbt("mod", [P, 96, 2])
    b_ada = sbt("b_ada_sb", [P, 96])
    silu_c = sbt("silu_c", [P, 2, KT])
    st = lambda n, k: sbt(n, [P, k])
    x_parts, x_ss, x_rstd = sbt("x_parts", [P, TT, 4]), st("x_ss", TT), st("x_rstd", TT)
    nhalf = st("nhalf", 16)
    head_ss, head_rstd = st("head_ss", 20), st("head_rstd", 20)
    q_rstd = [head_rstd[:, 12 * g:12 * g + 8].rearrange("p (t h) -> p t h", t=TT) for g in range(2)]
    k_rstd = head_rstd[:, 8:12].rearrange("p (t h) -> p t h", t=TT)
    sink = st("sink_sb", NQ)
    row_max, neg_max, sink_less = (sbt(n, [P, 2, TT, 4]) for n in ("row_max", "neg_max", "sink_less"))
    sums, sink_exp, r_den = (sbt(n, [P, 2, TT, 4]) for n in ("sums", "sink_exp", "r_den"))
    ln_stats = sbt("ln_stats", [P, TT, 2, 6])
    ln_mv = sbt("ln_mv", [P, TT, 2])
    ln_var, ln_rstd = st("ln_var", TT), st("ln_rstd", TT)
    half_ss = sbt("half_ss", [P, 2, TT, 2])
    half_sum = sbt("half_sum", [P, 2, TT])
    half_rstd = sbt("half_rstd", [P, 2, TT])

    table2 = sbt("table2", [P, 192])
    scale2 = sbt("scale2", [P, 3, KT])
    c_parts, c_ss, c_rstd = sbt("c_parts", [P, TT, 4]), st("c_ss", TT), st("c_rstd", TT)
    dt_b, a_log, d_res = st("dt_b", 32), st("a_log", 32), st("d_res", NH)
    filt = sbt("filt", [HY_HID, 3])
    not_first = st("not_first_sb", 1)
    ss2, rstd2 = sbt("ss2", [P, 2, 16]), sbt("rstd2", [P, 2, 16])

    in_h, U = sb("in_h", [P, KT, TOK], F32R)
    in_l = sbt("in_l", [P, KT, TOK], F32R)
    ARENA = base[0]
    a = ARENA

    def ar(name, shape, dtype=F32):
        nonlocal a
        r = sbt(name, shape, dtype, a)
        a += 4 * int(np.prod(shape[1:]))
        return r

    at_qk = a
    qk = ar("qk", [P, TT, 10, HD])
    attn = sbt("attn", [P, TT, 1024], at=at_qk)
    v_sb = ar("v_sb", [P, TT, NKV * HD])
    at_gv = a
    gv = ar("gv", [P, TT, 1024])
    gu = ar("gu", [P, TT, 1024])
    x_diag = sbt("x_diag", [P, TT, P], at=at_gv)
    rope_c = ar("rope_c", [P, 2, TT, 2, 64])
    rope_s = ar("rope_s", [P, 2, TT, 2, 64])
    gqk = ar("gqk", [P, 2, 2, 64])
    at_roped = a
    roped = ar("roped", [P, TT, 10, HD])
    at_qkT = a
    qkT = ar("qkT", [P, 10, TOK])
    gated = sbt("gated", [P, TT, 1024], at=at_qkT)
    at_s0 = a
    s0 = ar("scores0", [P, TT, 4, TOK])
    scores = [s0, sbt("scores1", [P, TT, 4, TOK], at=at_roped)]
    squares = sbt("squares", [P, TT, 4, HD], at=at_s0)
    ws_raw = sbt("ws_raw", [P, 8, P], at=at_s0)
    junk_attn = sbt("junk_attn", [P, CH], at=at_s0 + 4096)
    at_pT = a
    pT = ar("pT", [P, TT, 4, TT, P])
    rope_t = sbt("rope_t", [P, 2, TT, 4, 64], at=at_pT)
    ln_g = ar("ln_g", [P, 1024])
    ln_b = ar("ln_b", [P, 1024])
    wsT = ar("wsT", [P, 8, P])
    attn_end = a
    ah = sbt("ah", [P, FT, TOK], F32R, at=U)
    a = U + 4 * FT * TOK
    at_a = a
    act = ar("act", [P, FT, TOK])
    al = sbt("al", [P, FT, TOK], F32R, at=at_a)
    y = [ar(f"y{i}", [P, TT, CH]) for i in range(2)]
    cv = [ar(f"conv{i}", [P, 4, TOK]) for i in range(2)]
    a = max(a, attn_end)
    at_junk2 = a
    a += 4 * CH
    assert a <= nc.sbuf_usable_end, (a, nc.sbuf_usable_end)

    junk = sbt("junk", [P, CH], at=attn_end - 4 * 8 * P)
    at = lambda kb: U + int(kb * 1024)
    in_f = sbt("in_f", [P, KT, TOK], at=at(16))
    hc_h = sbt("hc_h", [P, KT, TOK], F32R, at(32))
    hc_f = sbt("hc_f", [P, KT, TOK], at=at(48))
    hc_l = sbt("hc_l", [P, KT, TOK], F32R, at(48))
    diag = sbt("diag", [P, 2, TT, P], at=at(64))
    ctx_first = sbt("ctx_first", [P, TT, D], at=at_s0)
    ada_raw = [sbt(f"ada_raw{i}", [P, 2, CH], at=at(32 + 4 * i)) for i in range(2)]
    ada_sum = [sbt("ada_sum0", [P, CH], at=at(108)), sbt("ada_sum1", [P, CH], at=at_junk2)]
    ada_term = [sbt(f"ada_term{i}", [P, CH], at=at(104 + 2 * i)) for i in range(2)]
    ada_last = [sbt(f"ada_last{i}", [P, CH], at=at(60 + 2 * i)) for i in range(2)]
    ctx_sb = sbt("ctx_sb", [P, TT, D], at=at(88))
    yB = [sbt(f"yB{i}", [P, TT, CH], at=at(66 + 4 * i)) for i in range(2)]
    cvB = [sbt(f"cvB{i}", [P, 4, TOK], at=at(74 + 4 * i)) for i in range(2)]
    yC = [sbt(f"yC{i}", [P, TT, CH], at=at(32 + 4 * i)) for i in range(2)]
    cvC = [sbt(f"cvC{i}", [P, 4, TOK], at=at(40 + 4 * i)) for i in range(2)]
    hy = [sbt(f"hy{i}", [P, TT, HYW], at=at(64 + 8 * i)) for i in range(3)]
    xs = [sbt(f"xs_{n}", [P, TT, SSW], at=at(88 + 8 * i)) for i, n in enumerate(("x", "ctx"))]
    zg = sbt("zg", [P, TT, SSW], at=at(96))
    states = sbt("states", [P, 2, SSW], at=at(104))
    bcT = sbt("bcT", [P, 4, TOK], at=at(48))
    b_ctx = sbt("b_ctx", [P, TT, TOK], at=at(52))
    dtn = [sbt(f"dt_{n}", [P, 4, 32], at=at(54 + i / 2)) for i, n in enumerate(
        ("raw", "abs", "exp", "w", "w2", "series", "relu", "dt", "da", "cum", "wc"))]
    dt_raw, dt_abs, dt_exp, dt_w, dt_w2, dt_q, dt_relu, dt_v, dt_da, dt_cum, dt_wc = dtn
    xw = [sbt(f"xw{i}", [P, TT, SSW], at=at(72 + 8 * i)) for i in range(2)]
    xdt = [sbt(f"xdt{i}", [P, TT, SSW], at=at(32 + 8 * i)) for i in range(2)]
    off_t = [sbt(f"off_t{i}", [P, CH], at=at(60 + 2 * i)) for i in range(2)]
    dlh = [sbt(f"dlh{i}", [P, 2, 3 * P], at=at(3 * i)) for i in range(2)]
    decays = [sbt(f"decays{i}", [P, 2, 3 * P], at=at(6 + 3 * i)) for i in range(2)]
    cbm = sbt("cbm", [P, 2, 2, 3 * P], at=at(12))
    h_sum = sbt("h_sum", [P, TT, HYW], at=at(0))
    h_0 = sbt("h_0", [P, TT, HYW], at=at(8))
    h_1 = sbt("h_1", [P, TT, HYW], at=at(16))
    h_abs = [sbt(f"h_abs{i}", [P, TT, HYW], at=at(96 + 8 * i)) for i in range(2)]
    r_norm = sbt("r_norm", [P, HYW], at=at(8))
    decay = sbt("decay_sb", [P, TT, HYW], at=at(24))
    K = [[sbt(f"K{o}{i}", [P, TT, HYW], at=at(32 + 16 * o + 8 * i)) for i in range(2)] for o in range(2)]
    Yf = [[sbt(f"Yf{c}{i}", [P, TT, CH], at=at(8 * c + 4 * i)) for i in range(2)] for c in range(2)]
    Yt = [sbt(f"Yt{i}", [P, CH], at=at(28 + 2 * i)) for i in range(2)]
    hy_t = sbt("hy_t", [P, TT, CH], at=at(28))
    hy_sq = sbt("hy_sq", [P, TT, HYW], at=at(0))
    hdn_a, hdn_n = sbt("hdn_a", [HY_HID, TOK], at=at(84)), sbt("hdn_n", [HY_HID, TOK], at=at(85))
    hdn = [sbt("hdn0", [HY_HID, TOK], at=at(86)), sbt("hdn1", [HY_HID, TOK], at=at(112))]
    feats = sbt("feats_sb", [HY_EMB, TOK], at=at(112))
    g_rows = [sbt(f"g_rows{i}", [P, D], at=at(96 + 8 * i)) for i in range(2)]
    g_diag = sbt("g_diag", [P, 4, P], at=at_junk2)
    hid_h = sbt("hid_h", [P, KT, TOK], F32R, at(32))
    hid_l = sbt("hid_l", [P, KT, TOK], F32R, at(48))
    y2 = [sbt(f"y2_{i}", [P, TT, CH], at=at(88 + 4 * i)) for i in range(2)]
    res_t = [sbt(f"res_t{i}", [P, TT, CH], at=at(80 + 4 * i)) for i in range(2)]
    f_norm = sbt("f_norm", [P, D], at=at(66))
    junk2 = sbt("junk2", [P, CH], at=at_junk2)
    masks = sbt("masks_sb", [P, 5, P], at=at_cos)
    fw1 = sbt("fw1", [HY_EMB, HY_HID], at=at_band + 1024)
    fw2 = sbt("fw2", [HY_HID, HY_HID], at=at_band + 1536)
    dft = sbt("dft_sb", [P, 2, TT, TOK], at=at_table)

    ps = lambda n: nc.alloc_psum_tensor(n, [P, CH], F32)
    acc = [[ps(f"acc{p}{i}") for i in range(TT)] for p in range(2)]
    tb = [ps(f"turn{i}") for i in range(2)]
    side = [ps("side0"), ps("side1")]

    sem = nc.alloc_semaphore
    w_loaded = [sem(f"w_loaded{s}") for s in range(NS)]
    w_hi = [sem(f"w_hi{s}") for s in range(NS)]
    w_lo = [sem(f"w_lo{s}") for s in range(NS)]
    w_free = [sem(f"w_free{s}") for s in range(NS)]
    acc_free = [sem(f"acc_free{p}") for p in range(2)]
    t_full = [sem(f"t_full{b}") for b in range(2)]
    t_free = [sem(f"t_free{b}") for b in range(2)]
    x_loaded, consts, staged_in, params = sem("x_loaded"), sem("consts"), sem("staged_in"), sem("params")
    cond_s, staged_clear, ctx_tick = sem("cond_s"), sem("staged_clear"), sem("ctx_tick")
    x_sq = sem("x_sq")
    stat, rstd = sem("stat"), sem("rstd")
    xn_ready, part_hi = sem("xn_ready"), sem("part_hi")
    roped_s, smax, expd, pT_s = sem("roped_s"), sem("smax"), sem("expd"), sem("pT_s")
    vn_s, gated_s, half_sq, half_s = sem("vn_s"), sem("gated_s"), sem("half_sq"), sem("half_s")
    wsT_s, qkT_s, attn_s = sem("wsT_s"), sem("qkT_s"), sem("attn_s")
    conv_id, silu_s, act_s = sem("conv_id"), sem("silu_s"), sem("act_s")
    ah_s, al_s = sem("ah_s"), sem("al_s")
    a_loaded = [sem(f"a_loaded{s}") for s in range(2)]
    a_used = sem("a_used")
    term_s, term_used = sem("term_s"), sem("term_used")
    ada_post, ada_mod = sem("ada_post"), sem("ada_mod")
    stored = sem("stored")
    staged2, params2, ctx_in, ssd_in, filt_in = sem("staged2"), sem("params2"), sem("ctx_in"), sem("ssd_in"), sem("filt_in")
    idft_in, fnorm_in, x_up = sem("idft_in"), sem("fnorm_in"), sem("x_up")
    decay_in, fw3_in = sem("decay_in"), sem("fw3_in")
    mt_used, y_done = sem("mt_used"), sem("y_done")
    diag_s, part2_hi, part2_lo = sem("diag_s"), sem("part2_hi"), sem("part2_lo")
    conv2_mid, bc_s = sem("conv2_mid"), sem("bc_s")
    dt_abs_s, dt_exp_s, da_s, cum_s = sem("dt_abs_s"), sem("dt_exp_s"), sem("da_s"), sem("cum_s")
    xw_s, dlh_s, mt_s = sem("xw_s"), sem("dlh_s"), sem("mt_s")
    side_full = [sem(f"side_full{b}") for b in range(2)]
    side_free = [sem(f"side_free{b}") for b in range(2)]
    gate2_s, ssd_sq, mix_s = sem("gate2_s"), sem("ssd_sq"), sem("mix_s")
    sin_arg, sin_s, filt_s, filtered = sem("sin_arg"), sem("sin_s"), sem("filt_s"), sem("filtered")
    abs_s = sem("abs_s")
    yf_s, conv_s, gdiag_s = sem("yf_s"), sem("conv_s"), sem("gdiag_s")
    hid_hi, hid_sq, final_s = sem("hid_hi"), sem("hid_sq"), sem("final_s")

    R_IN, R_O, R_UP, R_DN = 0, 7, 11, 11 + 2 * NPAIR
    RL = R_DN + 12
    U_TAB, U_N1, U_WS = 0, 2, 10
    U_QKA, U_QKB = 12, 16
    U_SA, U_SB, U_PA = 18, 22, 26
    U_VA, U_F, U_PB, U_VB = 30, 32, 36, 40
    U_AT, U_GT, U_N2, U_UP = 42, 46, 50, 58
    UL = U_UP + 4 * NPAIR
    assert UL % 2 == 0
    ADA_PIECES = KT // 2
    AL = [8 + 4 + 2 * NPAIR + 2, 8 + 4 + 2 * NPAIR + 6]
    DN_SIZES = [4] * 8 + [3] * 4
    DN_AT = [sum(DN_SIZES[:i]) for i in range(12)]
    IN_COLS = [0, 1024, 512, 2560, 3072, 1536, 2048]
    T_N1, T_N2, T_AO, T_GO, T_BS, T_CB, T_CW = 0, 16, 32, 40, 48, 56, 144

    def unit(l, u):
        return u % 2, l * (UL // 2) + u // 2 + 2

    def rnd(l, r):
        return l * RL + (r + 1)

    def rows(w, r0, n, c0, width=CH):
        return w[ds(r0, n * P), ds(c0, width)].rearrange("(k p) n -> p k n", p=P)

    w_in2 = t["w_in"].rearrange("l r n -> (l r) n")
    w_o2 = t["w_o"].rearrange("l r n -> (l r) n")
    w_up2 = t["w_up"].rearrange("l r n -> (l r) n")
    w_dn2 = t["w_down"].rearrange("l r n -> (l r) n")
    w_ada2 = t["w_ada_2"][0]

    def layer_rows(name, l, n):
        return t[name][ds(l, 1)].rearrange("o (r p) -> (o r) p", p=P)

    W_X, W_H, W_Z = 3 * HYW, 0, 3 * HYW + SSW + 512 + 32
    CHUNKS = [(W_X, 24, CH), (W_X + CH, 28, CH), (W_X + 2 * CH, 32, 256), (W_X + 3 * CH, None, 32)]
    CHUNKS += [(W_H + c * CH, 4 * c, 0) for c in range(6)] + [(W_Z + c * CH, None, 0) for c in range(2)]
    DT = 3
    SHARED = 4
    FIRST = [0, 4, 8, 12] + [13 + 5 * c for c in range(8)]
    OUT0 = FIRST[-1] + 5
    OUT = [(0, 2), (0, 3), (1, 2), (1, 3), (0, 0), (0, 1), (1, 0), (1, 1)] + [(c, k) for c in (2, 3) for k in range(4)]
    OUT_FIRST = [min(n for n in range(16) if OUT[n][0] == c) for c in range(4)]
    OUT_LAST = [max(n for n in range(16) if OUT[n][0] == c) for c in range(4)]
    MLP0 = OUT0 + 16
    s_hyb, s_fw = (OUT0 + 2) % NS, (OUT0 + 3) % NS
    hy_b = sbt("hy_b", [P, 2, HYW], at=at_raw[s_hyb])
    fw3 = [sbt(f"fw3_{o}", [HY_HID, 2 * HYW], at=(at_raw, at_hi)[o][s_fw]) for o in range(2)]
    idft = sbt("idft_sb", [P, 2, TT, TOK], at=at_hi[s_hyb])
    R2 = rnd(2, 0)
    ADA2 = {FIRST[j] + 2: (22 + (j - SHARED) // 4, (j - SHARED) % 4) for j in range(SHARED, 12)}

    def pieces_of(j):
        return [(FIRST[j] + i, q) for i, q in enumerate([0] if j == DT else range(4) if j < SHARED else (0, 1, None, 2, 3))]

    def ring(n, q=0):
        return n % NS, q * 8 + (R2 + n // NS)

    def numbered(names, first):
        return {n: (i % 2, first + i // 2) for i, n in enumerate(names)}

    HY_CH = range(SHARED, SHARED + 6)
    conv_jobs = [(n, s) for n in range(3) for s in "xc"] + [(n, "x") for n in HY_CH]
    tiles_of = lambda job: 2 if job == (2, "c") else 4

    def back_units(job):
        return 0 if job == (2, "x") else 1 if job == (2, "c") else 2

    order = ["tab", "tab2"] + [("ctx", i) for i in range(8)] + [("x", i) for i in range(8)]
    for n in list(range(3)) + list(HY_CH):
        streams = "xc" if n < 3 else "x"
        order += [("F", n, s, u) for s in streams for u in range(tiles_of((n, s)) // 2)]
        order += ["f1"] if n == 6 else []
        order += [("B", n, s, u) for s in streams for u in range(back_units((n, s)))]
        order += ["f2"] if n == 6 else []
    order += [("E", h, d) for h in range(NH) for d in range(2)]
    order += [("g", i) for i in range(8)]
    order += [("ssd", i) for i in range(4)] + [("hy", i) for i in range(4)] + [("n2", i) for i in range(8)]
    UNITS = numbered(order, UL + 2)
    assert len(order) % 2 == 0
    MLP_U = UL + 2 + len(order) // 2

    uses = [[], []]
    for n in range(SHARED):
        uses[0].append(("in", n, "x"))
        uses[1].append(("in", n, "c"))
    for n in range(SHARED, 12):
        uses[n % 2].append(("in", n, "x"))
    for g in range(2):
        uses[g].append(("y", g))
    for o in range(2):
        for i in range(4):
            uses[i % 2].append(("h", o, i))
        for c in range(2):
            for p in range(2):
                uses[p].append(("K", o, c, p))
    for o in range(2):
        for c in range(2):
            for p in range(2):
                uses[p].append(("Z", o, c, p))
    for c in range(4):
        uses[c % 2].append(("out", c))
    USES = {u: (p, 2 * AL[p] + 1 + i) for p in range(2) for i, u in enumerate(uses[p])}
    MLP_A = [2 * AL[p] + 1 + len(uses[p]) for p in range(2)]

    side_uses = [[], []]
    for b in range(2):
        side_uses[b] += (["cum"], [])[b] + [("state", d) for d in range(2)] + ([("ada", 22), ("ada", 23)], [])[b] + ["CB"] + [("off", g, i) for g in range(2) for i in range(TT)]
        side_uses[b] += [("norm", o) for o in range(2)] + [("conv", o, c) for o in range(2) for c in range(2)]
    SIDE = [{u: k for k, u in enumerate(side_uses[b])} for b in range(2)]

    w_in_b, w_out_b = t["w_in_2"][0], t["w_out_2"][0]
    w1_b, w2_b = t["w_mlp1_2"][0], t["w_mlp2_2"][0]

    V_N1, V_N2, V_HY, V_SSD, V_CB, V_CW = 0, 16, 32, 40, 48, 84

    def dt_view(w):
        return w[:, 0].rearrange("p (k n) -> p k n", n=32)

    def conv_buffers(n, s):
        return (yB["xc".index(s)], cvB["xc".index(s)]) if n < 3 else (yC[n % 2], cvC[n % 2])

    def conv_dest(n, s, i):
        if n < 2:
            return xs["xc".index(s)][:, i, n * CH:(n + 1) * CH]
        return hy[(n - SHARED) // 2][:, i, (n % 2) * CH:(n % 2 + 1) * CH]

    block_guard = nc.Block()
    block = block_guard.__enter__()

    @block.sync
    def _(sp):
        def piece(src, s, r, n=4):
            sp.wait_ge(w_free[s], r)
            sp.dma_start(raw[s][:, 0:n], src).then_inc(w_loaded[s], 16)

        sp.dma_start(x_sb[:], t["x"][0].rearrange("(t p) d -> p t d", p=P)).then_inc(x_loaded, 16)
        for dst, name in ((ident, "ident"), (cos, "cos"), (sin, "sin"), (band, "band")):
            sp.dma_start(dst[:], t[name]).then_inc(consts, 16)
        sp.wait_ge(staged_clear, 1)
        for r0, n, src in ((0, 16, t["c_2"][0]), (16, 16, t["c_ctx_2"])):
            sp.dma_start(staged[r0:r0 + n, 0], src.rearrange("(r p) -> r p", p=P)).then_inc(staged_in, 16)
        sp.dma_start(staged[0:96, 1], t["b_ada_2"][0].rearrange("(r p) -> r p", p=P)).then_inc(staged_in, 16)
        sp.dma_start(ctx_first[:], t["ctx_2"][0].rearrange("(t p) d -> p t d", p=P)).then_inc(x_loaded, 16)
        with sp.Fori(0, 2) as l:
            for b in range(2):
                sp.wait_ge(t_full[b], l * (UL // 2) + 1)
            r0 = 0
            for name, n in (("norm1_g", 16), ("norm2_g", 16), ("attn_out_g", 8), ("sgu_out_g", 8)):
                sp.dma_start(staged[r0:r0 + n, 0], layer_rows(name, l, n)).then_inc(staged_in, 16)
                r0 += n
            sp.dma_start(staged[r0:r0 + 8, 0], t["b_s"][ds(l, 1)].rearrange("o h p -> (o h) p")).then_inc(staged_in, 16)
            sp.dma_start(staged[0:88, 1], layer_rows("conv_b", l, 88)).then_inc(staged_in, 16)
            for k in range(3):
                src = t["conv_w"].rearrange("l k n -> (l k) n")[ds(l * 3 + k, 1)].rearrange("o (r p) -> (o r) p", p=P)
                sp.dma_start(staged[0:88, 2 + k], src).then_inc(staged_in, 16)
            for c, col in enumerate(IN_COLS):
                for s in range(NS):
                    piece(rows(w_in2, l * D + s * CH, 4, col), s, rnd(l, R_IN + c))
                if c == 0:
                    for dst, src in (
                        (gqk[:, 0], t["q_norm_g"][ds(l, 1)]), (gqk[:, 1], t["k_norm_g"][ds(l, 1)]),
                    ):
                        sp.dma_start(dst, src.rearrange("o (h d) -> o h d", h=2).to_broadcast([P, 2, 64])).then_inc(params, 16)
                    for dst, name, n in ((sink, "sink", NQ), (ln_g, "sgu_ln_g", 1024), (ln_b, "sgu_ln_b", 1024)):
                        sp.dma_start(dst[:], t[name][ds(l, 1)].to_broadcast([P, n])).then_inc(params, 16)
                    sp.wait_ge(x_sq, 16)
                    sp.dma_start(ws_raw[:], t["w_s"][ds(l, 1)].rearrange("o h p q -> p (o h) q")).then_inc(params, 16)
            with sp.Fori(0, 4) as c:
                for s in range(NS):
                    piece(rows(w_o2, l * D + s * CH, 4, c * CH), s, rnd(l, R_O) + c)
            with sp.Fori(0, NPAIR) as j:
                rb = sp.snap(rnd(l, R_UP) + j * 2)
                for n in range(8):
                    piece(rows(w_up2, l * D + n % 4 * CH, 4, j * CH + n // 4 * DFF), n % NS, rb + n // NS)
            with sp.Fori(0, 4) as c:
                rb = sp.snap(rnd(l, R_DN) + c * 3)
                for i, n in enumerate(DN_SIZES):
                    piece(rows(w_dn2, l * DFF + DN_AT[i] * P, n, c * CH), i % NS, rb + i // NS, n)
        sp.wait_ge(act_s, 2 * NPAIR + 1)
        sp.dma_start(ctx_sb[:], t["ctx_2"][0].rearrange("(t p) d -> p t d", p=P)).then_inc(ctx_in, 16)
        sp.wait_ge(t_full[0], unit(1, U_TAB)[1])
        sp.wait_ge(t_full[1], unit(1, U_TAB + 1)[1])
        r0 = 0
        for name, n in (("norm1_w_2", 16), ("norm2_w_2", 16), ("hy_norm_w_2", 8), ("ssd_norm_w_2", 8), ("hy_conv_b_2", 24), ("ssd_conv_b_2", 12)):
            sp.dma_start(staged[r0:r0 + n, 0], t[name][0].rearrange("(r p) -> r p", p=P)).then_inc(staged2, 16)
            r0 += n
        for k in range(3):
            for name, r0, n in (("hy_conv_w_2", 36 * k, 24), ("ssd_conv_w_2", 36 * k + 24, 12)):
                sp.dma_start(staged[r0:r0 + n, 1], t[name][0, k].rearrange("(r p) -> r p", p=P)).then_inc(staged2, 16)
        def piece2(n, src):
            s, r = ring(n)
            piece(src, s, r)

        for k in range(2):
            piece2(k, rows(w_in_b, k * CH, 4, CHUNKS[0][0]))
        sp.dma_start(dt_b[:], t["dt_bias_2"].rearrange("o d h -> o (d h)").to_broadcast([P, 32])).then_inc(params2, 16)
        sp.dma_start(a_log[:], t["a_log_2"].rearrange("o d h -> o (d h)").to_broadcast([P, 32])).then_inc(params2, 16)
        sp.dma_start(d_res[:], t["ssd_d_2"].to_broadcast([P, NH])).then_inc(params2, 16)
        sp.dma_start(not_first[:], t["not_first"]).then_inc(filt_in, 16)
        for i, name in enumerate(("filt_freq_2", "filt_b1_2", "filt_b2_2")):
            sp.dma_start(filt[:, i:i + 1], t[name].rearrange("o p -> p o")).then_inc(filt_in, 16)
        sp.dma_start(masks[:], t["masks"]).then_inc(params2, 16)
        sp.dma_start(fw1[:], t["filt_w1_2"][0]).then_inc(filt_in, 16)
        sp.dma_start(fw2[:], t["filt_w2_2"][0]).then_inc(filt_in, 16)
        for j, (col, _, _) in enumerate(CHUNKS):
            if j == DT:
                s, r = ring(FIRST[j])
                sp.wait_ge(w_free[s], r)
                sp.dma_start(dt_view(raw[s]), w_in_b[:, col:col + 32].rearrange("(k p) n -> p k n", p=P)).then_inc(w_loaded[s], 16)
                for u in ("tab", "tab2"):
                    sp.wait_ge(t_free[UNITS[u][0]], UNITS[u][1] + 1)
                sp.dma_start(dft[:], t["dft"]).then_inc(filt_in, 16)
                sp.dma_start(feats[:], t["feats"]).then_inc(filt_in, 16)
                continue
            for n, s in pieces_of(j):
                if n < 2:
                    continue
                if s is None:
                    i, k = ADA2[n]
                    piece2(n, rows(w_ada2, k * CH, 4, i * CH))
                else:
                    piece2(n, rows(w_in_b, s * CH, 4, col))
        def out_piece(n):
            c, k = OUT[n]
            piece2(OUT0 + n, rows(w_out_b, k * CH, 4, c * CH))

        for n in range(2):
            out_piece(n)
        sp.wait_ge(w_free[ring(OUT0 + 2)[0]], ring(OUT0 + 2)[1])
        sp.dma_start(hy_b[:], t["hy_bias_2"].rearrange("o a n -> o (a n)").to_broadcast([P, 2 * HYW]).rearrange("p (a n) -> p a n", a=2)).then_inc(idft_in, 16)
        sp.wait_ge(w_free[ring(OUT0 + 3)[0]], ring(OUT0 + 3)[1])
        sp.dma_start(decay[:], t["decay"]).then_inc(decay_in, 16)
        for o in range(2):
            sp.dma_start(fw3[o][:], t["filt_w3_2"][0][:, o * 2 * HYW:(o + 1) * 2 * HYW]).then_inc(fw3_in, 16)
        sp.dma_start(idft[:], t["idft"]).then_inc(idft_in, 16)
        sp.wait_ge(conv_s, 4)
        for n in range(2, 16):
            out_piece(n)
            if n == 8:
                sp.dma_start(f_norm[:], t["final_norm_w_2"].rearrange("(o n) -> o n", o=1).to_broadcast([P, D])).then_inc(fnorm_in, 16)
        with sp.Fori(0, 4) as q:
            r = sp.snap(q * 8 + R2)
            for n in range(32):
                c, k = n // NS % 4, n % NS
                if n < 16:
                    src = rows(w1_b, k * CH, 4, q * D + c * CH)
                else:
                    src = rows(w2_b, q * D + k * CH, 4, c * CH)
                piece(src, (MLP0 + n) % NS, r + (MLP0 + n) // NS)
        for i in range(TT):
            for c in range(4):
                sp.wait_ge(final_s, 4 * i + c + 1)
                sp.dma_start(out[0, i * P:(i + 1) * P, c * CH:(c + 1) * CH], x_sb[:, i, c * CH:(c + 1) * CH]).then_inc(stored, 16)
        sp.wait_ge(stored, 16 * 8)

    @block.gpsimd
    def _(pool):
        def root(k, dst, src, width):
            pool.wait_ge(stat, k)
            nc.gpsimd.tensor_tensor(dst, src, nhalf[:, 0:width], ALU.pow).then_inc(rstd, 1)

        def ctx_sums(i):
            m = pool.snap(i * KT)
            for k in range(KT):
                if k == 0:
                    pool.wait_ge(ada_mod, i + 1)
                    pool.sem_inc(ctx_tick, 1)
                pool.wait_ge(term_s, m + (k + 1))
                if k == 0:
                    nc.gpsimd.tensor_tensor(ada_sum[1][:], ada_term[0][:], zero[:].to_broadcast([P, CH]), ALU.add).then_inc(term_used, 1)
                else:
                    nc.gpsimd.tensor_tensor(ada_sum[1][:], ada_sum[1][:], ada_term[k % 2][:], ALU.add).then_inc(term_used, 1)
                pool.drain()

        nc.gpsimd.memset(nhalf[:], -0.5)
        nc.gpsimd.memset(one[:], 1.0)
        nc.gpsimd.memset(zero[:], 0.0)
        pool.drain()
        pool.sem_inc(ctx_tick, 1)
        pool.wait_ge(cond_s, 1)
        with pool.Fori(0, 2) as l:
            s7 = pool.snap(l * 7)
            root(s7 + 1, x_rstd[:], x_ss[:], TT)
            root(s7 + 2, head_rstd[:, 0:12], head_ss[:, 0:12], 12)
            root(s7 + 3, head_rstd[:, 12:20], head_ss[:, 12:20], 8)
            root(s7 + 4, ln_rstd[:], ln_var[:], TT)
            root(s7 + 5, half_rstd[:, 0], half_sum[:, 0], TT)
            root(s7 + 6, half_rstd[:, 1], half_sum[:, 1], TT)
            root(s7 + 7, x_rstd[:], x_ss[:], TT)
            with pool.Fori(0, NPAIR) as j:
                ctx_sums(l * NPAIR + j)

        root(15, c_rstd[:], c_ss[:], TT)
        root(16, x_rstd[:], x_ss[:], TT)
        root(17, rstd2[:, 0, 0:4], ss2[:, 0, 0:4], 4)
        root(18, rstd2[:, 1], ss2[:, 1], 16)
        root(19, x_rstd[:], x_ss[:], TT)
        root(20, x_rstd[:], x_ss[:], TT)

    @block.scalar
    def _(act_):
        def split_hi(s, r, n=4):
            act_.wait_ge(w_loaded[s], r * 16)
            nc.scalar.activation(hi[s][:, 0:n], raw[s][:, 0:n], ACT.Copy).then_inc(w_hi[s], 1)

        def gained_hi(l, u0, kt0, n, col):
            for i in range(n // 2):
                b, k = unit(l, u0 + i)
                act_.wait_ge(t_full[b], k)
                for j in range(2):
                    kt = 2 * i + j
                    nc.scalar.activation(in_h[:, kt0 + kt], tb[b][:, j * TOK:(j + 1) * TOK], ACT.Copy,
                                         scale=table[:, col + kt:col + kt + 1]).then_inc(part_hi, 1)

        def square_sum(src, dst):
            a = nc.scalar.activation(junk[:], src, ACT.Square, accum_out=dst)
            act_.drain()
            return a

        def half_square_sum(src, dst):
            a = nc.scalar.activation(junk_attn[:], src, ACT.Square, accum_out=dst)
            act_.drain()
            return a

        def x_squares(count, p, c):
            act_.drain()
            act_.wait_ge(acc_free[p], count)
            for i in range(TT):
                square_sum(x_sb[:, i, ds(c * CH, CH)], x_parts[:, i, ds(c, 1)]).then_inc(x_sq, 1)

        act_.wait_ge(t_full[0], 1)
        nc.scalar.activation(silu_c[:].rearrange("p a k -> p (a k)"), tb[0][:, 0:32], ACT.Silu).then_inc(t_free[0], 1)
        act_.drain().then_inc(cond_s, 1)
        act_.wait_ge(x_loaded, 16)
        for i in range(TT):
            for c in range(4):
                square_sum(x_sb[:, i, c * CH:(c + 1) * CH], x_parts[:, i, c:c + 1]).then_inc(x_sq, 1)
        split_hi(0, 1)
        split_hi(1, 1)
        act_.wait_ge(x_loaded, 32)
        for i in range(TT):
            for c in range(4):
                square_sum(ctx_first[:, i, c * CH:(c + 1) * CH], c_parts[:, i, c:c + 1]).then_inc(x_sq, 1)

        with act_.Fori(0, 2) as l:
            act_.wait_ge(t_full[0], unit(l, U_TAB)[1])
            nc.scalar.activation(table[:, 0:T_CB], tb[0][:, 0:T_CB], ACT.Copy)
            nc.scalar.activation(table[:, T_CB:T_CW], tb[0][:, P:P + 88], ACT.Copy).then_inc(t_free[0], 1)
            act_.wait_ge(t_full[1], unit(l, U_TAB)[1])
            nc.scalar.activation(table[:, T_CW:].rearrange("p (k f) -> p k f", k=3),
                                 tb[1][:, 0:3 * P].rearrange("p (k f) -> p k f", k=3)[:, :, 0:88], ACT.Copy).then_inc(t_free[1], 1)
            act_.drain()
            gained_hi(l, U_N1, 0, KT, T_N1)

            a0 = l * AL[0] + 1
            for c in range(7):
                p = c % 2
                r = act_.snap(rnd(l, R_IN + c))
                split_hi(2, r)
                split_hi(3, r)
                if c == 1:
                    for i in range(2):
                        b, k = unit(l, U_WS + i)
                        act_.wait_ge(t_full[b], k)
                        nc.scalar.activation(wsT[:, 4 * i:4 * i + 4].rearrange("p h q -> p (h q)"), tb[b][:], ACT.Copy).then_inc(t_free[b], 1)
                if c == 4:
                    for i in range(TT):
                        b, k = unit(l, U_QKB + i)
                        act_.wait_ge(t_full[b], k)
                        nc.scalar.activation(qkT[:, 4:8, i * P:(i + 1) * P], tb[b][:].rearrange("p (h q) -> p h q", h=4), ACT.Copy).then_inc(t_free[b], 1)
                if c in (5, 6):
                    g = c - 5
                    act_.wait_ge(smax, l * 2 + g + 1)
                    for i in range(TT):
                        for h in range(4):
                            nc.scalar.activation(scores[g][:, i, h], scores[g][:, i, h], ACT.Exp,
                                                 bias=neg_max[:, g, i, h:h + 1], accum_out=sums[:, g, i, h:h + 1])
                    nc.scalar.activation(sink_exp[:, g], sink_less[:, g], ACT.Exp)
                    act_.drain().then_inc(expd, 1)
                split_hi(0, r + 1)
                if c == 3:
                    for i in range(TT):
                        b, k = unit(l, U_QKA + i)
                        act_.wait_ge(t_full[b], k)
                        nc.scalar.activation(qkT[:, 0:4, i * P:(i + 1) * P], tb[b][:].rearrange("p (h q) -> p h q", h=4), ACT.Copy).then_inc(t_free[b], 1)
                split_hi(1, r + 1)
                if c == 3:
                    for i in range(TT):
                        b, k = unit(l, U_QKA + 2 + i)
                        act_.wait_ge(t_full[b], k)
                        nc.scalar.activation(qkT[:, 8:10, i * P:(i + 1) * P], tb[b][:, 0:256].rearrange("p (h q) -> p h q", h=2), ACT.Copy).then_inc(t_free[b], 1)
                if c == 5:
                    for i in range(4):
                        b, k = unit(l, U_PA + i)
                        act_.wait_ge(t_full[b], k)
                        nc.scalar.activation(pT[:, i // 2, 2 * (i % 2):2 * (i % 2) + 2].rearrange("p h k q -> p (h k q)"), tb[b][:], ACT.Copy).then_inc(t_free[b], 1)
                act_.wait_ge(w_free[3], r + 1)
                for i in range(TT):
                    src = acc[p][i]
                    if c == 1:
                        nc.scalar.activation(qk[:, i, 8:10].rearrange("p h d -> p (h d)"), src[:, 0:256], ACT.Copy).then_inc(acc_free[p], 1)
                        nc.scalar.activation(v_sb[:, i], src[:, 256:512], ACT.Copy).then_inc(acc_free[p], 1)
                    elif c < 3:
                        nc.scalar.activation(qk[:, i, 2 * c:2 * c + 4].rearrange("p h d -> p (h d)"), src[:], ACT.Copy).then_inc(acc_free[p], 1)
                    else:
                        dst = gv if c < 5 else gu
                        o = CH * ((c - 3) % 2)
                        nc.scalar.activation(dst[:, i, o:o + CH], src[:], ACT.Gelu_apprx_tanh).then_inc(acc_free[p], 1)
                if c == 6:
                    for i in range(4):
                        b, k = unit(l, U_PB + i)
                        act_.wait_ge(t_full[b], k)
                        nc.scalar.activation(pT[:, i // 2, 2 * (i % 2):2 * (i % 2) + 2].rearrange("p h k q -> p (h k q)"), tb[b][:], ACT.Copy).then_inc(t_free[b], 1)
            act_.drain()
            act_.wait_ge(attn_s, l * 2 + 2)
            for i in range(TT):
                for g in range(2):
                    half_square_sum(attn[:, i, g * CH:(g + 1) * CH], half_ss[:, 0, i, g:g + 1])
            act_.drain().then_inc(half_sq, 1)
            act_.wait_ge(gated_s, l + 1)
            for i in range(TT):
                for g in range(2):
                    half_square_sum(gated[:, i, g * CH:(g + 1) * CH], half_ss[:, 1, i, g:g + 1])
            act_.drain().then_inc(half_sq, 1)
            gained_hi(l, U_AT, 0, 8, T_AO)
            gained_hi(l, U_GT, 8, 8, T_GO)

            with act_.Fori(0, 2) as cp:
                for q in range(2):
                    r = act_.snap(rnd(l, R_O + q) + cp * 2)
                    split_hi(2, r)
                    split_hi(3, r)
                    split_hi(0, r + 1)
                    split_hi(1, r + 1)
                    x_squares(l * AL[q] + cp * 2 + (1 + 8 + 2), q, cp * 2 + q)
            gained_hi(l, U_N2, 0, KT, T_N2)

            def centre(j, c):
                tk = l * (UL // 2) + j * 2 + (U_UP // 2 + 2 + c)
                for u in range(2):
                    act_.wait_ge(t_full[u], tk)
                    if c == 0 and u == 0:
                        act_.wait_ge(act_s, l * NPAIR + j + 1)
                    for f in range(2 * u, 2 * u + 2):
                        at = j * 4 + (44 * c + f)
                        nc.scalar.activation(cv[c][:, f], tb[u][:, (f % 2) * TOK:(f % 2 + 1) * TOK], ACT.Identity,
                                             scale=table[:, ds(at + (T_CW + 88), 1)], bias=table[:, ds(at + T_CB, 1)]).then_inc(conv_id, 1)

            def up_pair(j, before):
                r = act_.snap(rnd(l, R_UP) + j * 2)
                i = act_.snap(l * NPAIR + j)
                m = act_.snap(i * KT)
                ra = act_.snap(i * (ADA_PIECES // 2))
                tk = act_.snap(l * (UL // 2) + j * 2 + (U_UP // 2 + 2))

                def split_up(n):
                    split_hi(n % NS, r + n // NS)

                def load_ada(n):
                    act_.wait_ge(a_used, i * ADA_PIECES + (n + 1))
                    act_.dma_start(ada_raw[n % 2][:], rows(w_ada2, n * 2 * P, 2, i * CH)).then_inc(a_loaded[n % 2], 16)

                def ctx_terms(n):
                    act_.wait_ge(a_loaded[n % 2], ra * 16 + 16 * (n // 2 + 1))
                    for k in range(2):
                        act_.wait_ge(term_used, m + (2 * n + k + 1))
                        nc.scalar.activation(ada_term[k][:], ada_raw[n % 2][:, k], ACT.Copy,
                                             scale=silu_c[:, 1, 2 * n + k:2 * n + k + 1]).then_inc(term_s, 1)
                    act_.drain()

                load_ada(0)
                load_ada(1)
                split_up(2)
                if before is not None:
                    centre(before, 1)
                split_up(3)
                ctx_terms(0)
                split_up(4)
                load_ada(2)
                ctx_terms(1)
                split_up(5)
                load_ada(3)
                ctx_terms(2)
                act_.wait_ge(w_free[3], r + 1)
                for k in range(TT):
                    nc.scalar.activation(y[0][:, k], acc[0][k][:], ACT.Copy).then_inc(acc_free[0], 1)
                split_up(6)
                load_ada(4)
                ctx_terms(3)
                centre(j, 0)
                split_up(7)
                load_ada(5)
                ctx_terms(4)
                for u in range(2):
                    act_.wait_ge(t_free[u], tk + 1)
                nc.scalar.activation(cv[0][:], cv[0][:], ACT.Silu).then_inc(silu_s, 1)
                split_up(8)
                load_ada(6)
                ctx_terms(5)
                split_up(9)
                load_ada(7)
                ctx_terms(6)
                ctx_terms(7)
                act_.wait_ge(w_free[3], r + 2)
                for k in range(TT):
                    nc.scalar.activation(y[1][:, k], acc[1][k][:], ACT.Copy).then_inc(acc_free[1], 1)

            up_pair(0, None)
            with act_.Fori(1, NPAIR) as j:
                up_pair(j, act_.snap(j + (-1)))
            for i in range(12):
                k, n = DN_AT[i], DN_SIZES[i]
                if i == 1:
                    centre(NPAIR - 1, 1)
                if i == 0:
                    act_.wait_ge(act_s, l * NPAIR + NPAIR)
                if k + n > FT - 4 and DN_AT[i - 1] + DN_SIZES[i - 1] <= FT - 4:
                    act_.wait_ge(act_s, l * NPAIR + NPAIR + 1)
                nc.scalar.activation(ah[:, k:k + n], act[:, k:k + n], ACT.Copy).then_inc(ah_s, 1)
                m = i + 2
                if m < 12:
                    split_hi(m % NS, rnd(l, R_DN + m // NS), DN_SIZES[m])
            r = act_.snap(rnd(l, R_DN + 3))
            split_hi(0, r)
            split_hi(1, r)
            x_squares(l * AL[0] + (1 + 8 + 4 + 2 * NPAIR + 2), 0, 0)
            with act_.Fori(1, 4) as c:
                r = act_.snap(rnd(l, R_DN) + c * 3)
                for i in range(2, 14):
                    split_hi(i % NS, r + i // NS, (DN_SIZES + [4, 4])[i])
                x_squares(l * AL[1] + c * 2 + (1 + 8 + 4 + 2 * NPAIR), 1, c)

        def split_hi2(n, q=0):
            s, r = ring(n, q)
            act_.wait_ge(w_loaded[s], r * 16)
            if n == FIRST[DT]:
                nc.scalar.activation(dt_view(hi[s]), dt_view(raw[s]), ACT.Copy).then_inc(w_hi[s], 1)
            else:
                nc.scalar.activation(hi[s][:], raw[s][:], ACT.Copy).then_inc(w_hi[s], 1)

        def whole_hi(names, full, dst):
            for i, u in enumerate(names):
                b, k = UNITS[u]
                act_.wait_ge(t_free[b], k + 1)
                nc.scalar.activation(dst[:, 2 * i:2 * i + 2], full[:, 2 * i:2 * i + 2], ACT.Copy).then_inc(part2_hi, 1)

        def square_sum2(src, dst):
            a = nc.scalar.activation(junk2[:], src, ACT.Square, accum_out=dst)
            act_.drain()
            return a

        def centre2(n, s):
            cv_ = conv_buffers(n, s)[1]
            for u in range(tiles_of((n, s)) // 2):
                b, k = UNITS["F", n, s, u]
                act_.wait_ge(t_full[b], k)
                for f in range(2 * u, 2 * u + 2):
                    v = CHUNKS[n][1] + f
                    a = nc.scalar.activation(cv_[:, f], tb[b][:, (f % 2) * TOK:(f % 2 + 1) * TOK], ACT.Identity,
                                             scale=table2[:, V_CW + 36 + v:V_CW + 37 + v], bias=table2[:, V_CB + v:V_CB + v + 1])
                a.then_inc(conv2_mid, 1)

        def back2(n, s):
            for i in range(back_units((n, s))):
                b, k = UNITS["B", n, s, i]
                act_.wait_ge(t_full[b], k)
                if (n, s) == (2, "c"):
                    nc.scalar.activation(b_ctx[:].rearrange("p t n -> p (t n)"), tb[b][:], ACT.Silu).then_inc(t_free[b], 1)
                else:
                    nc.scalar.activation(conv_dest(n, s, i), tb[b][:], ACT.Silu if n < 3 else ACT.Copy).then_inc(t_free[b], 1)

        for u, at_, n in (("tab", V_N1, V_CW), ("tab2", V_CW, 108)):
            b, k = UNITS[u]
            act_.wait_ge(t_full[b], k)
            nc.scalar.activation(table2[:, at_:at_ + n], tb[b][:, 0:n], ACT.Copy).then_inc(t_free[b], 1)
        whole_hi([("ctx", i) for i in range(8)], hc_f, hc_h)
        whole_hi([("x", i) for i in range(8)], in_f, in_h)
        for j in range(12):
            for n, s in pieces_of(j):
                if n + 2 not in ADA2:
                    split_hi2(n + 2)
                if s is None:
                    continue
                if j in (1, 2):
                    (centre2, back2)[s // 2](j - 1, "xc"[s % 2])
                if j > SHARED and j <= SHARED + 6 and s % 2 == 0:
                    (centre2, back2)[s // 2](j - 1, "x")
                if j == SHARED and s < 2:
                    centre2(2, "xc"[s])
                if (j, s) == (SHARED, 1):
                    for u in range(2):
                        b, k = UNITS["F", 2, "x", u]
                        act_.wait_ge(t_free[b], k + 1)
                    nc.scalar.activation(bcT[:], cvB[0][:], ACT.Silu).then_inc(bc_s, 1)
                if (j, s) == (SHARED, 2):
                    act_.wait_ge(params2, 64)
                    nc.scalar.activation(a_log[:], a_log[:], ACT.Exp)
                    act_.wait_ge(dt_abs_s, 1)
                    nc.scalar.activation(dt_exp[:], dt_abs[:], ACT.Exp, scale=-1.0).then_inc(dt_exp_s, 1)
                if (j, s) == (SHARED, 3):
                    back2(2, "c")
                if (j, s) == (SHARED + 1, 1):
                    act_.wait_ge(side_full[0], SIDE[0]["cum"] + 1)
                    nc.scalar.activation(dt_cum[:].rearrange("p t h -> p (t h)"), side[0][:, 0:P], ACT.Exp).then_inc(side_free[0], 1)
                if j == SHARED + 2 and s % 2 == 1:
                    for g in range(2):
                        act_.wait_ge(side_full[g], SIDE[g]["state", s // 2] + 1)
                        nc.scalar.activation(states[:, s // 2, g * CH:(g + 1) * CH], side[g][:], ACT.Copy).then_inc(side_free[g], 1)
                if (j, s) in ((SHARED + 3, 2), (SHARED + 4, 0)):
                    i = j - SHARED - 3
                    act_.wait_ge(sin_arg, i + 1)
                    nc.scalar.activation(hdn[i][:], hdn_a[:], ACT.Sin).then_inc(sin_s, 1)
            if j == DT:
                continue
            sl, r = ring(pieces_of(j)[-1][0])
            act_.wait_ge(w_free[sl], r + 1)
            for st_ in ("xc" if j < SHARED else "x"):
                p, k = USES["in", j, st_]
                for i in range(TT):
                    if j >= SHARED + 6:
                        o = (j - SHARED - 6) * CH
                        a = nc.scalar.activation(zg[:, i, o:o + CH], acc[p][i][:], ACT.Silu)
                    else:
                        cols = 256 if (j, st_) == (2, "c") else CH
                        a = nc.scalar.activation(conv_buffers(j, st_)[0][:, i, 0:cols], acc[p][i][:, 0:cols], ACT.Copy)
                a.then_inc(acc_free[p], 1)

        for g in range(2):
            with act_.Fori(0, 4) as hp:
                for m in range(2):
                    h = act_.snap(hp * 2 + (8 * g + m))
                    for d in range(2):
                        b, k = UNITS["E", 0, d]
                        if d == 0:
                            act_.wait_ge(mt_used, h + 1)
                        act_.wait_ge(t_full[b], h + k)
                        nc.scalar.activation(decays[m][:, d], tb[b][:, 0:3 * P], ACT.Exp).then_inc(t_free[b], 1)
        act_.wait_ge(gate2_s, 1)
        for i in range(TT):
            for g in range(2):
                square_sum2(xs[0][:, i, g * CH:(g + 1) * CH], ss2[:, 0, 2 * i + g:2 * i + g + 1])
        act_.drain().then_inc(ssd_sq, 1)
        for o in range(2):
            for i in range(4):
                d, ch = i // 2, slice(i % 2 * CH, (i % 2 + 1) * CH)
                p, k = USES["h", o, i]
                act_.wait_ge(acc_free[p], k + 1)
                if i == 0 and o > 0:
                    act_.wait_ge(side_full[1], SIDE[1]["norm", o - 1] + 1)
                nc.scalar.activation(h_abs[d][:, :, ch], (h_0, h_1)[d][:, :, ch], ACT.Abs).then_inc(abs_s, 1)
        for i in range(8):
            kt = (32, 80)[i // 4] + 4 * (i % 4)
            for f in range(4):
                a = nc.scalar.activation(g_diag[:, f], ident[:], ACT.Copy, scale=mod[:, kt + f, 0:1])
            a.then_inc(gdiag_s, 1)
            b, k = UNITS["g", i]
            act_.wait_ge(t_full[b], k)
            nc.scalar.activation(g_rows[i // 4][:, (i % 4) * CH:(i % 4 + 1) * CH], tb[b][:], ACT.Copy).then_inc(t_free[b], 1)
        for name, kt0, col in (("ssd", 8, V_SSD), ("hy", 0, V_HY)):
            if name == "hy":
                for n in (2, 3):
                    split_hi2(OUT0 + n)
            for i in range(4):
                b, k = UNITS[name, i]
                act_.wait_ge(t_full[b], k)
                for f in range(2):
                    kt = 2 * i + f
                    a = nc.scalar.activation(in_h[:, kt0 + kt], tb[b][:, f * TOK:(f + 1) * TOK], ACT.Copy, scale=table2[:, col + kt:col + kt + 1])
                a.then_inc(part2_hi, 1)
        def x_squares2(count, c):
            act_.wait_ge(x_up, count)
            for i in range(TT):
                square_sum2(x_sb[:, i, c * CH:(c + 1) * CH], x_parts[:, i, c:c + 1]).then_inc(x_sq, 1)

        for n in range(16):
            if n >= 2:
                split_hi2(OUT0 + n + 2)
            if n in OUT_LAST:
                x_squares2(OUT_LAST.index(n) + 1, OUT_LAST.index(n))
        whole_hi([("n2", i) for i in range(8)], in_f, in_h)

        def hidden(q, last):
            kq = q * 4 if last else act_.snap(q * 4)
            xq = None if last else 0
            for n in range(32):
                if not (last and n >= 30):
                    s = (MLP0 + n + 2) % NS
                    r = ring(MLP0 + n + 2, q)[1]
                    act_.wait_ge(w_loaded[s], r * 16)
                    nc.scalar.activation(hi[s][:], raw[s][:], ACT.Copy).then_inc(w_hi[s], 1)
                if n % NS == 1 and 1 <= n // NS <= 4:
                    c = n // NS - 1
                    for u in range(2):
                        act_.wait_ge(t_full[u], kq + (MLP_U + c))
                        nc.scalar.activation(hid_h[:, 4 * c + 2 * u:4 * c + 2 * u + 2].rearrange("p k n -> p (k n)"), tb[u][:], ACT.Copy).then_inc(hid_hi, 1)
                if n < 16 and n % NS == 3:
                    p = n // NS % 2
                    act_.wait_ge(w_free[(MLP0 + n) % NS], ring(MLP0 + n, q)[1] + 1)
                    for i in range(TT):
                        a = nc.scalar.activation(y2[p][:, i], acc[p][i][:], ACT.Relu)
                    a.then_inc(acc_free[p], 1)
                if last and n >= 16 and n % NS == 3:
                    x_squares2(4 + 4 * q + (n - 16) // NS + 1, (n - 16) // NS)

        with act_.Fori(0, 3) as q:
            hidden(q, False)
        hidden(3, True)

    @block.vector
    def _(dve):
        def split_lo(s, r, n=4):
            dve.wait_ge(w_hi[s], r)
            nc.vector.tensor_tensor(lo[s][:, 0:n], raw[s][:, 0:n], hi[s][:, 0:n].bitcast(F32), ALU.subtract).then_inc(w_lo[s], 1)

        def gained_lo(l, u0, kt0, n, col, h0):
            for i in range(n // 2):
                b, k = unit(l, u0 + i)
                dve.wait_ge(part_hi, l * 48 + (h0 + 2 * i + 2))
                for j in range(2):
                    kt = 2 * i + j
                    last = nc.vector.scalar_tensor_tensor(
                        in_l[:, kt0 + kt], tb[b][:, j * TOK:(j + 1) * TOK], table[:, col + kt:col + kt + 1],
                        in_h[:, kt0 + kt].bitcast(F32), ALU.mult, ALU.subtract)
                last.then_inc(t_free[b], 1)

        def normalise(l, k, sq):
            dve.wait_ge(x_sq, sq)
            nc.vector.tensor_reduce(x_ss[:], x_parts[:], X_AXIS, ALU.add)
            dve.drain()
            nc.vector.tensor_scalar(x_ss[:], x_ss[:], 1.0 / D, EPS, ALU.mult, ALU.add).then_inc(stat, 1)
            dve.wait_ge(rstd, l * 7 + k)
            for i in range(TT):
                nc.vector.tensor_scalar(x_diag[:, i], ident[:], x_rstd[:, i:i + 1], None, ALU.mult).then_inc(xn_ready, 1)

        def modulate(i):
            dve.wait_ge(ada_post, i + 1)
            nc.vector.tensor_tensor(mod[:, ds(i * 4, 4)], side[0][:, 0:8].rearrange("p (f c) -> p f c", c=2),
                                    b_ada[:, ds(i * 4, 4)].unsqueeze(2).to_broadcast([P, 4, 2]), ALU.add).then_inc(ada_mod, 1)

        def add_to_x(r, s, p, c):
            dve.wait_ge(w_free[s], r + 1)
            for i in range(TT):
                at = x_sb[:, i, ds(c * CH, CH)]
                nc.vector.tensor_tensor(at, at, acc[p][i][:], ALU.add).then_inc(acc_free[p], 1)

        nc.vector.memset(staged[:], 0.0).then_inc(staged_clear, 1)
        for s in range(NS):
            dve.sem_inc(w_free[s], 1)
        for s in (*acc_free, *t_free, act_s, ada_mod):
            dve.sem_inc(s, 1)
        for s, n in ((a_used, 2), (term_used, 2)):
            dve.sem_inc(s, n)
        dve.wait_ge(t_full[1], 1)
        nc.vector.tensor_copy(b_ada[:], tb[1][:, 0:96]).then_inc(t_free[1], 1)
        split_lo(0, 1)
        split_lo(1, 1)
        dve.wait_ge(cond_s, 1)

        def c_sums(dst, src, k0, n):
            for k in range(n):
                c = silu_c[:, 0, k0 + k:k0 + k + 1]
                if k0 + k == 0:
                    a = nc.vector.tensor_scalar(dst[:], src[:, k], c, None, ALU.mult)
                else:
                    a = nc.vector.scalar_tensor_tensor(dst[:], src[:, k], c, dst[:], ALU.mult, ALU.add)
                if k < n - 1:
                    dve.drain()
            return a

        dve.wait_ge(consts, 64)
        with dve.Fori(0, 2) as l:
            normalise(l, 1, l * 24 + 8)
            gained_lo(l, U_N1, 0, KT, T_N1, 0)

            a0, a1 = l * AL[0] + 1, l * AL[1] + 1

            def head_sums(heads, n, at, scale, bias):
                ss = head_ss[:, at:at + TT * n]
                nc.vector.tensor_tensor(squares[:, :, 0:n], qk[:, :, heads:heads + n], qk[:, :, heads:heads + n], ALU.mult)
                dve.drain()
                nc.vector.tensor_reduce(ss.rearrange("p (t h) -> p t h", t=TT), squares[:, :, 0:n], X_AXIS, ALU.add)
                dve.drain()
                return nc.vector.tensor_scalar(ss, ss, scale, bias, ALU.mult, ALU.add)

            def rope(heads, n, which):
                src = lambda h: qk[:, :, heads:heads + n, 64 * h:64 * h + 64]
                dst = lambda h: roped[:, :, heads:heads + n, 64 * h:64 * h + 64]
                coef = lambda tab, h: tab[:, which, :, h].unsqueeze(2).to_broadcast([P, TT, n, 64])
                for h in range(2):
                    nc.vector.tensor_tensor(dst(h), src(h), coef(rope_c, h), ALU.mult)
                    nc.vector.tensor_tensor(rope_t[:, h, :, 0:n], src(1 - h), coef(rope_s, h), ALU.mult)
                dve.drain()
                for h in range(2):
                    last = nc.vector.tensor_tensor(dst(h), dst(h), rope_t[:, h, :, 0:n], ALU.add)
                return last

            def scale_scores(g, i):
                for u in range(2):
                    b, k = unit(l, (U_SA, U_SB)[g] + 2 * i + u)
                    dve.wait_ge(t_full[b], k)
                    for h in range(2):
                        last = nc.vector.scalar_tensor_tensor(
                            scores[g][:, i, 2 * u + h], tb[b][:, h * TOK:(h + 1) * TOK], q_rstd[g][:, i, 2 * u + h:2 * u + h + 1],
                            band[:, i], ALU.mult, ALU.add)
                    last.then_inc(t_free[b], 1)

            def maxima(g):
                sk = sink[:, 4 * g:4 * g + 4].unsqueeze(1).to_broadcast([P, TT, 4])
                dve.drain()
                nc.vector.tensor_reduce(row_max[:, g], scores[g][:], X_AXIS, ALU.max)
                dve.drain()
                nc.vector.tensor_tensor(row_max[:, g], row_max[:, g], sk, ALU.max)
                dve.drain()
                nc.vector.tensor_scalar(neg_max[:, g], row_max[:, g], -1.0, None, ALU.mult)
                nc.vector.tensor_tensor(sink_less[:, g], sk, row_max[:, g], ALU.subtract)
                dve.drain().then_inc(smax, 1)

            def denominators(g):
                dve.wait_ge(expd, l * 2 + g + 1)
                nc.vector.tensor_tensor(sums[:, g], sums[:, g], sink_exp[:, g], ALU.add)
                dve.drain()
                nc.vector.reciprocal(r_den[:, g], sums[:, g])
                dve.drain()

            def attended(g):
                for i in range(TT):
                    b, k = unit(l, (U_VA, U_VB)[g] + i)
                    dve.wait_ge(t_full[b], k)
                    nc.vector.tensor_tensor(attn[:, i, g * CH:(g + 1) * CH].rearrange("p (h d) -> p h d", h=4),
                                            tb[b][:].rearrange("p (h d) -> p h d", h=4),
                                            r_den[:, g, i].unsqueeze(2).to_broadcast([P, 4, HD]), ALU.mult).then_inc(t_free[b], 1)
                dve.drain().then_inc(attn_s, 1)

            def spatial(i):
                for u in range(2):
                    b, k = unit(l, U_F + 2 * i + u)
                    dve.wait_ge(t_full[b], k)
                    nc.vector.tensor_tensor(gated[:, i, u * CH:(u + 1) * CH].rearrange("p (h d) -> p h d", h=4),
                                            tb[b][:].rearrange("p (h d) -> p h d", h=4),
                                            table[:, T_BS + 4 * u:T_BS + 4 * u + 4].unsqueeze(2).to_broadcast([P, 4, HD]), ALU.add).then_inc(t_free[b], 1)

            for c in range(7):
                r = dve.snap(rnd(l, R_IN + c))
                split_lo(2, r)
                if c == 1:
                    dve.wait_ge(params, l * 96 + 96)
                    for w in range(2):
                        nc.vector.tensor_tensor(rope_c[:, w], cos[:].unsqueeze(2).to_broadcast([P, TT, 2, 64]),
                                                gqk[:, w].unsqueeze(1).to_broadcast([P, TT, 2, 64]), ALU.mult)
                        for h in range(2):
                            nc.vector.tensor_tensor(rope_s[:, w, :, h], sin[:, :, h],
                                                    gqk[:, w, 1 - h].unsqueeze(1).to_broadcast([P, TT, 64]), ALU.mult)
                if c == 2:
                    dve.wait_ge(acc_free[1], a1 + 4)
                    dve.wait_ge(acc_free[0], a0 + 2)
                    head_sums(8, 2, 8, 1.0 / HD, EPS)
                    dve.drain()
                    head_sums(0, 4, 0, 1.0, HD * EPS).then_inc(stat, 1)
                if c == 3:
                    dve.wait_ge(acc_free[0], a0 + 4)
                    head_sums(4, 4, 12, 1.0, HD * EPS).then_inc(stat, 1)
                if c == 6:
                    dve.wait_ge(rstd, l * 7 + 4)
                    for i in range(TT):
                        nc.vector.tensor_scalar(gv[:, i], gv[:, i], ln_mv[:, i, 0:1], ln_rstd[:, i:i + 1], ALU.subtract, ALU.mult)
                    dve.drain()
                    nc.vector.tensor_tensor(gv[:], gv[:], ln_g[:].unsqueeze(1).to_broadcast([P, TT, 1024]), ALU.mult)
                    dve.drain()
                    nc.vector.tensor_tensor(gv[:], gv[:], ln_b[:].unsqueeze(1).to_broadcast([P, TT, 1024]), ALU.add).then_inc(vn_s, 1)
                split_lo(3, r)
                if c == 2:
                    rope(0, 4, 0).then_inc(roped_s, 1)
                if c == 3:
                    rope(4, 4, 0).then_inc(roped_s, 1)
                if c == 5:
                    dve.wait_ge(rstd, l * 7 + 3)
                    scale_scores(1, 0)
                if c == 6:
                    denominators(0)
                    attended(0)
                split_lo(0, r + 1)
                if c == 2:
                    dve.wait_ge(rstd, l * 7 + 2)
                    nc.vector.tensor_tensor(qk[:, :, 8:10], qk[:, :, 8:10], k_rstd.unsqueeze(3).to_broadcast([P, TT, 2, HD]), ALU.mult)
                    dve.drain()
                    rope(8, 2, 1).then_inc(roped_s, 1)
                if c == 4:
                    dve.wait_ge(rstd, l * 7 + 2)
                    scale_scores(0, 0)
                if c == 5:
                    scale_scores(1, 1)
                if c == 6:
                    spatial(0)
                split_lo(1, r + 1)
                if c == 4:
                    scale_scores(0, 1)
                    maxima(0)
                if c == 5:
                    maxima(1)
                    dve.wait_ge(acc_free[0], a0 + 6)
                    dve.wait_ge(acc_free[1], a1 + 6)
                    for i in range(TT):
                        for h in range(2):
                            nc.vector.bn_stats(ln_stats[:, i, h], gv[:, i, h * CH:(h + 1) * CH])
                    dve.drain()
                    for i in range(TT):
                        nc.vector.bn_aggr(ln_mv[:, i], ln_stats[:, i])
                    dve.drain()
                    nc.vector.tensor_scalar(ln_var[:], ln_mv[:, :, 1], 1.0, EPS, ALU.mult, ALU.add).then_inc(stat, 1)
                if c == 6:
                    spatial(1)
            denominators(1)
            attended(1)
            dve.drain()
            dve.wait_ge(acc_free[1], a1 + 8)
            dve.wait_ge(acc_free[0], a0 + 8)
            nc.vector.tensor_tensor(gated[:], gated[:], gu[:], ALU.mult).then_inc(gated_s, 1)
            for m in range(2):
                dve.wait_ge(half_sq, l * 2 + m + 1)
                nc.vector.tensor_reduce(half_sum[:, m], half_ss[:, m], X_AXIS, ALU.add)
                dve.drain()
                nc.vector.tensor_scalar(half_sum[:, m], half_sum[:, m], 1.0 / 1024, EPS, ALU.mult, ALU.add).then_inc(stat, 1)
                dve.wait_ge(rstd, l * 7 + (5 + m))
                src = (attn, gated)[m]
                for i in range(TT):
                    nc.vector.tensor_scalar(src[:, i], src[:, i], half_rstd[:, m, i:i + 1], None, ALU.mult).then_inc(half_s, 1)
            gained_lo(l, U_AT, 0, 8, T_AO, 16)
            gained_lo(l, U_GT, 8, 8, T_GO, 24)

            with dve.Fori(0, 2) as cp:
                for q in range(2):
                    r = dve.snap(rnd(l, R_O + q) + cp * 2)
                    split_lo(2, r)
                    split_lo(3, r)
                    split_lo(0, r + 1)
                    split_lo(1, r + 1)
                    add_to_x(r, 3, q, cp * 2 + q)
            normalise(l, 7, l * 16 + 24)
            gained_lo(l, U_N2, 0, KT, T_N2, 32)

            def outer_taps(j, c):
                cid = dve.snap(l * (8 * NPAIR) + j * 8)
                for u in range(2):
                    dve.wait_ge(conv_id, cid + (4 * c + 2 * u + 2))
                    for f in range(2 * u, 2 * u + 2):
                        h = tb[u][:, (f % 2) * TOK:(f % 2 + 1) * TOK]
                        w = table[:, ds(j * 4 + (44 * c + f + T_CW), 1)]
                        nc.vector.scalar_tensor_tensor(cv[c][:, f, 1:TOK], h[:, 0:TOK - 1], w, cv[c][:, f, 1:TOK], ALU.mult, ALU.add)
                    dve.drain()
                    for f in range(2 * u, 2 * u + 2):
                        h = tb[u][:, (f % 2) * TOK:(f % 2 + 1) * TOK]
                        w = table[:, ds(j * 4 + (44 * c + f + T_CW + 176), 1)]
                        last = nc.vector.scalar_tensor_tensor(cv[c][:, f, 0:TOK - 1], h[:, 1:TOK], w, cv[c][:, f, 0:TOK - 1], ALU.mult, ALU.add)
                    last.then_inc(t_free[u], 1)

            def finish_pair(j):
                outer_taps(j, 1)
                dve.drain()
                dve.wait_ge(silu_s, l * NPAIR + j + 1)
                nc.vector.tensor_tensor(act[:, ds(j * 4, 4)], cv[0][:], cv[1][:], ALU.mult).then_inc(act_s, 1)
                modulate(l * NPAIR + j)

            def up_pair(j, before):
                r = dve.snap(rnd(l, R_UP) + j * 2)
                ra = dve.snap((l * NPAIR + j) * (ADA_PIECES // 2))

                def split_up(i):
                    split_lo(i % NS, r + i // NS)

                def ada_piece(n):
                    dve.drain()
                    dve.wait_ge(a_loaded[n % 2], ra * 16 + 16 * (n // 2 + 1))
                    c_sums(ada_sum[0], ada_raw[n % 2], 2 * n, 2).then_inc(a_used, 1)

                split_up(2)
                if before is not None:
                    finish_pair(before)
                split_up(3)
                ada_piece(0)
                split_up(4)
                ada_piece(1)
                split_up(5)
                ada_piece(2)
                split_up(6)
                ada_piece(3)
                outer_taps(j, 0)
                split_up(7)
                ada_piece(4)
                split_up(8)
                ada_piece(5)
                split_up(9)
                ada_piece(6)
                ada_piece(7)

            up_pair(0, None)
            with dve.Fori(1, NPAIR) as j:
                up_pair(j, dve.snap(j + (-1)))
            for i in range(12):
                k, n = DN_AT[i], DN_SIZES[i]
                dve.wait_ge(ah_s, l * 12 + i + 1)
                nc.vector.tensor_tensor(al[:, k:k + n], act[:, k:k + n], ah[:, k:k + n].bitcast(F32), ALU.subtract).then_inc(al_s, 1)
                if i == 1:
                    finish_pair(NPAIR - 1)
                m = i + 2
                if m < 12:
                    split_lo(m % NS, rnd(l, R_DN + m // NS), DN_SIZES[m])
            r = dve.snap(rnd(l, R_DN + 3))
            split_lo(0, r)
            split_lo(1, r)
            add_to_x(r - 1, 3, 0, 0)
            with dve.Fori(1, 4) as c:
                r = dve.snap(rnd(l, R_DN) + c * 3)
                for i in range(2, 14):
                    if i == 13:
                        add_to_x(r + 2, 3, 1, c)
                    split_lo(i % NS, r + i // NS, (DN_SIZES + [4, 4])[i])

        def split_lo2(n):
            s, r = ring(n)
            dve.wait_ge(w_hi[s], r)
            v = dt_view if n == FIRST[DT] else lambda w: w[:]
            nc.vector.tensor_tensor(v(lo[s]), v(raw[s]), v(hi[s]).bitcast(F32), ALU.subtract).then_inc(w_lo[s], 1)

        def diagonal(which, r):
            for i in range(TT):
                a = nc.vector.tensor_scalar(diag[:, which, i], ident[:], r[:, i:i + 1], None, ALU.mult)
            a.then_inc(diag_s, 1)

        def x_norm(sq, k):
            dve.drain()
            dve.wait_ge(x_sq, sq)
            nc.vector.tensor_reduce(x_ss[:], x_parts[:], X_AXIS, ALU.add)
            dve.drain()
            nc.vector.tensor_scalar(x_ss[:], x_ss[:], 1.0 / D, EPS, ALU.mult, ALU.add).then_inc(stat, 1)
            dve.wait_ge(rstd, k)

        def whole(names, full, low, high, which, shift, done):
            def low_part(i):
                dve.wait_ge(part2_hi, done + i + 1)
                two = slice(2 * i, 2 * i + 2)
                nc.vector.tensor_tensor(low[:, two], full[:, two], high[:, two].bitcast(F32), ALU.subtract).then_inc(part2_lo, 1)

            for i, u in enumerate(names):
                b, k = UNITS[u]
                dve.wait_ge(t_full[b], k)
                for f in range(2):
                    kt = 2 * i + f
                    a = nc.vector.tensor_scalar(full[:, kt], tb[b][:, f * TOK:(f + 1) * TOK], scale2[:, which, kt:kt + 1],
                                                shift(kt), ALU.mult, ALU.add)
                a.then_inc(t_free[b], 1)
                if i > 0:
                    low_part(i - 1)
            low_part(len(names) - 1)

        def taps2(n, s):
            cv_ = conv_buffers(n, s)[1]
            seg = SEG if s == "x" else TOK
            mids = sum(tiles_of(j) // 2 for j in conv_jobs[:conv_jobs.index((n, s))])
            for u in range(tiles_of((n, s)) // 2):
                b, _ = UNITS["F", n, s, u]
                dve.drain()
                dve.wait_ge(conv2_mid, mids + u + 1)
                for k in (0, 2):
                    for f in range(2 * u, 2 * u + 2):
                        h = tb[b][:, (f % 2) * TOK:(f % 2 + 1) * TOK].rearrange("p (a b) -> p a b", b=seg)
                        o = cv_[:, f].rearrange("p (a b) -> p a b", b=seg)
                        w = table2[:, V_CW + 36 * k + CHUNKS[n][1] + f:V_CW + 36 * k + CHUNKS[n][1] + f + 1]
                        o, h = (o[:, :, 1:seg], h[:, :, 0:seg - 1]) if k == 0 else (o[:, :, 0:seg - 1], h[:, :, 1:seg])
                        a = nc.vector.scalar_tensor_tensor(o, h, w, o, ALU.mult, ALU.add)
                    if k == 0:
                        dve.drain()
                a.then_inc(t_free[b], 1)

        def step_widths():
            sl, r = ring(FIRST[DT])
            dve.wait_ge(params2, 64)
            dve.wait_ge(w_free[sl], r + 1)
            for m, s in enumerate("xc"):
                p, _ = USES["in", DT, s]
                for i in range(TT):
                    a = nc.vector.tensor_tensor(dt_raw[:, 2 * m + i], acc[p][i][:, 0:32], dt_b[:], ALU.add)
                a.then_inc(acc_free[p], 1)
            dve.drain()
            nc.vector.tensor_scalar(dt_abs[:], dt_raw[:], -1.0, None, ALU.mult)
            nc.vector.tensor_scalar(dt_relu[:], dt_raw[:], 0.0, None, ALU.max)
            dve.drain()
            nc.vector.tensor_tensor(dt_abs[:], dt_abs[:], dt_raw[:], ALU.max).then_inc(dt_abs_s, 1)

        def step_logs():
            dve.wait_ge(dt_exp_s, 1)
            nc.vector.tensor_scalar(dt_w[:], dt_exp[:], 2.0, None, ALU.add)
            dve.drain()
            nc.vector.reciprocal(dt_w[:], dt_w[:])
            dve.drain()
            nc.vector.tensor_tensor(dt_w[:], dt_w[:], dt_exp[:], ALU.mult)
            dve.drain()
            nc.vector.tensor_tensor(dt_w2[:], dt_w[:], dt_w[:], ALU.mult)
            dve.drain()
            nc.vector.tensor_scalar(dt_q[:], dt_w2[:], 1.0 / 19, None, ALU.mult)
            for k in range(8, 0, -1):
                dve.drain()
                nc.vector.scalar_tensor_tensor(dt_q[:], dt_q[:], 1.0 / (2 * k + 1), dt_w2[:], ALU.add, ALU.mult)
            dve.drain()
            nc.vector.scalar_tensor_tensor(dt_w[:], dt_q[:], 1.0, dt_w[:], ALU.add, ALU.mult)
            dve.drain()
            nc.vector.scalar_tensor_tensor(dt_v[:], dt_w[:], 2.0, dt_relu[:], ALU.mult, ALU.add)
            dve.drain()
            nc.vector.scalar_tensor_tensor(dt_da[:], dt_v[:], -1.0, a_log[:].unsqueeze(1).to_broadcast([P, 4, 32]), ALU.mult, ALU.mult).then_inc(da_s, 1)

        def by_head(x):
            return x.rearrange("p t (h w) -> p t h w", w=PH)

        def per_head(x):
            return x.unsqueeze(3).to_broadcast([P, TT, NH, PH])

        nc.vector.tensor_reduce(c_ss[:], c_parts[:], X_AXIS, ALU.add)
        dve.drain()
        nc.vector.tensor_scalar(c_ss[:], c_ss[:], 1.0 / D, EPS, ALU.mult, ALU.add).then_inc(stat, 1)
        for u in ("tab", "tab2"):
            dve.wait_ge(t_free[UNITS[u][0]], UNITS[u][1] + 1)
        dve.drain()
        for m, (kt, c, v) in enumerate(((16, 0, V_N1), (16, 1, V_N1), (64, 0, V_N2))):
            nc.vector.scalar_tensor_tensor(scale2[:, m], mod[:, kt:kt + KT, c], 1.0, table2[:, v:v + KT], ALU.add, ALU.mult)
        dve.wait_ge(rstd, 15)
        diagonal(1, c_rstd)
        x_norm(48, 16)
        diagonal(0, x_rstd)
        whole([("ctx", i) for i in range(8)], hc_f, hc_l, hc_h, 1, lambda kt: mod[:, kt, 1:2], 0)
        whole([("x", i) for i in range(8)], in_f, in_l, in_h, 0, lambda kt: mod[:, kt, 0:1], 8)
        dve.sem_inc(mt_used, 2)
        def sine_argument(i):
            turns = 1.0 / (2 * math.pi)
            c1 = 6.28125
            c2 = float(np.float32(2 * math.pi - c1))
            c3 = 2 * math.pi - c1 - c2
            b, k = UNITS[f"f{i + 1}"]
            dve.wait_ge(filt_in, 16 * 8)
            dve.wait_ge(t_full[b], k)
            nc.vector.tensor_scalar(hdn_a[:], tb[b][0:HY_HID, 0:TOK], filt[:, i + 1:i + 2], filt[:, 0:1], ALU.add, ALU.mult).then_inc(t_free[b], 1)
            dve.drain()
            nc.vector.tensor_scalar(hdn_n[:], hdn_a[:], turns, 12582912.0, ALU.mult, ALU.add)
            dve.drain()
            nc.vector.tensor_scalar(hdn_n[:], hdn_n[:], 12582912.0, None, ALU.subtract)
            for c_ in (c1, c2, c3):
                dve.drain()
                nc.vector.scalar_tensor_tensor(hdn_a[:], hdn_n[:], -c_, hdn_a[:], ALU.mult, ALU.add)
            dve.drain()
            nc.vector.tensor_scalar(hdn_a[:], hdn_a[:], 3.1415925, -3.1415925, ALU.min, ALU.max).then_inc(sin_arg, 1)

        def last_modulation(i):
            dve.wait_ge(side_full[0], SIDE[0]["ada", i] + 1)
            nc.vector.tensor_tensor(mod[:, 4 * i:4 * i + 4, 0], side[0][:, 0:4], b_ada[:, 4 * i:4 * i + 4], ALU.add).then_inc(side_free[0], 1)

        for j in range(12):
            for n, s in pieces_of(j):
                if n + 2 in ADA2:
                    i, q = ADA2[n + 2]
                    sl, r = ring(n + 2)
                    dve.wait_ge(w_loaded[sl], r * 16)
                    c_sums(ada_last[i - 22], raw[sl], 4 * q, 4).then_inc(w_hi[sl], 1)
                    dve.drain().then_inc(w_lo[sl], 1)
                    dve.sem_inc(w_free[sl], 1)
                else:
                    split_lo2(n + 2)
                if s is None:
                    continue
                if (j, s) == (SHARED + 4, 3):
                    last_modulation(22)
                if (j, s) in ((SHARED + 3, 2), (SHARED + 4, 0)):
                    sine_argument(j - SHARED - 3)
                if j in (1, 2) and s < 2:
                    taps2(j - 1, "xc"[s])
                if j == SHARED and s < 2:
                    taps2(2, "xc"[s])
                if (j, s) == (SHARED, 3):
                    step_logs()
                if SHARED < j <= SHARED + 6 and s == 0:
                    taps2(j - 1, "x")
                if (j, s) == (SHARED + 1, 3):
                    dve.wait_ge(side_free[0], SIDE[0]["cum"] + 1)
                    nc.vector.tensor_tensor(dt_wc[:, 0:2], dt_cum[:, 2:4], dt_v[:, 2:4], ALU.mult)
                    dve.drain()
                    for d in range(2):
                        nc.vector.tensor_tensor(by_head(xw[d]), by_head(xs[1]), per_head(dt_wc[:, 0:2, d * NH:(d + 1) * NH]), ALU.mult).then_inc(xw_s, 1)
                if (j, s) == (11, 1):
                    b, k = UNITS["B", 9, "x", 1]
                    dve.wait_ge(t_free[b], k + 1)
                    for d in range(2):
                        nc.vector.tensor_tensor(by_head(xdt[d]), by_head(xs[0]), per_head(dt_v[:, 0:2, d * NH:(d + 1) * NH]), ALU.mult)
                    nc.vector.tensor_tensor(by_head(xs[0]), by_head(xs[0]),
                                            d_res[:].unsqueeze(1).to_broadcast([P, TT, NH]).unsqueeze(3).to_broadcast([P, TT, NH, PH]), ALU.mult)
            if j == DT:
                step_widths()

        last_modulation(23)
        LE, GT, ONES, LT, GE = range(5)
        for g in range(2):
            dve.wait_ge(side_full[g], SIDE[g]["CB"] + 1)
            for d, blocks in enumerate((((0, 0, LE), (0, 1, None), (1, 1, LE)), ((1, 0, None), (1, 1, GE), (0, 0, GE)))):
                for n, (si, li, m) in enumerate(blocks):
                    o = cbm[:, g, d, n * P:(n + 1) * P]
                    src = side[g][:, si * TOK + li * P:si * TOK + (li + 1) * P]
                    if m is None:
                        a = nc.vector.tensor_copy(o, src)
                    else:
                        a = nc.vector.tensor_tensor(o, src, masks[:, m], ALU.mult)
            a.then_inc(side_free[g], 1)
        def head_steps(h, m):
            step = lambda i, d: dt_da[:, i, ds(h + d * NH, 1)]
            nc.vector.tensor_scalar(dlh[m][:, 0, 0:P], masks[:, GT], step(0, 0), None, ALU.mult)
            nc.vector.tensor_scalar(dlh[m][:, 0, P:], masks[:, GT:ONES + 1].rearrange("p m q -> p (m q)"), step(1, 0), None, ALU.mult)
            nc.vector.tensor_scalar(dlh[m][:, 1, 0:P], masks[:, LT], step(1, 1), None, ALU.mult)
            nc.vector.tensor_scalar(dlh[m][:, 1, P:], masks[:, ONES:LT + 1].rearrange("p m q -> p (m q)"), step(0, 1), None, ALU.mult).then_inc(dlh_s, 1)

        def head_products(h, g, m):
            for d in range(2):
                b, k = UNITS["E", 0, d]
                dve.wait_ge(t_free[b], h + (k + 1))
            nc.vector.tensor_tensor(decays[m][:], decays[m][:], cbm[:, g], ALU.mult).then_inc(mt_s, 1)

        head_steps(0, 0)
        for g in range(2):
            dve.drain()
            with dve.Fori(0, 4 - g) as hp:
                head_steps(dve.snap(hp * 2 + (8 * g + 1)), 1)
                head_products(dve.snap(hp * 2 + 8 * g), g, 0)
                head_steps(dve.snap(hp * 2 + (8 * g + 2)), 0)
                head_products(dve.snap(hp * 2 + (8 * g + 1)), g, 1)
            if g == 1:
                head_steps(NH - 1, 1)
                head_products(NH - 2, g, 0)
                head_products(NH - 1, g, 1)
        for g in range(2):
            for i in range(TT):
                ch = slice(g * CH, (g + 1) * CH)
                for d in range(2):
                    dve.wait_ge(side_full[d], SIDE[d]["off", g, i] + 1)
                    nc.vector.tensor_tensor(off_t[d][:].rearrange("p (h w) -> p h w", w=PH), side[d][:].rearrange("p (h w) -> p h w", w=PH),
                                            dt_cum[:, i, d * NH + 8 * g:d * NH + 8 * g + 8].unsqueeze(2).to_broadcast([P, 8, PH]), ALU.mult).then_inc(side_free[d], 1)
                for d in range(2):
                    dve.drain()
                    nc.vector.tensor_tensor(xs[0][:, i, ch], xs[0][:, i, ch], off_t[d][:], ALU.add)
                dve.drain()
                dve.wait_ge(y_done, g + 1)
                a = nc.vector.tensor_tensor(xs[0][:, i, ch], xs[0][:, i, ch], acc[g][i][:], ALU.add)
            a.then_inc(acc_free[g], 1)
        dve.drain()
        nc.vector.tensor_tensor(xs[0][:], xs[0][:], zg[:], ALU.mult).then_inc(gate2_s, 1)

        dve.wait_ge(decay_in, 16)
        for o in range(2):
            for i in range(4):
                d, c = i // 2, i % 2
                p, _ = USES["h", o, i]
                ch = slice(c * CH, (c + 1) * CH)
                dve.wait_ge(filt_s, 6 * o + i + 1)
                for tt in range(TT):
                    h = (h_0, h_1)[d]
                    if d == 1 and tt == 0:
                        a = nc.vector.scalar_tensor_tensor(h[:, tt, ch], acc[p][tt][:], not_first[:], decay[:, tt, ch], ALU.mult, ALU.mult)
                    else:
                        a = nc.vector.tensor_tensor(h[:, tt, ch], acc[p][tt][:], decay[:, tt, ch], ALU.mult)
                a.then_inc(acc_free[p], 1)
            dve.drain()
            nc.vector.tensor_tensor(h_sum[:], h_0[:], h_1[:], ALU.add)
            dve.wait_ge(abs_s, 4 * o + 4)
            nc.vector.tensor_tensor(h_1[:], h_1[:], h_0[:], ALU.subtract).then_inc(filtered, 1)
            dve.drain()
            if o == 0:
                dve.wait_ge(ssd_sq, 1)
                nc.vector.tensor_scalar(ss2[:, 0, 0:4], ss2[:, 0, 0:4], 1.0 / 512, EPS, ALU.mult, ALU.add).then_inc(stat, 1)
                dve.wait_ge(rstd, 17)
                y_groups = xs[0][:].rearrange("p t (g w) -> p (t g) w", w=CH)
                nc.vector.tensor_tensor(y_groups, y_groups, rstd2[:, 0, 0:4].unsqueeze(2).to_broadcast([P, 4, CH]), ALU.mult).then_inc(mix_s, 1)
            for c in range(2):
                dve.wait_ge(side_full[c], SIDE[c]["norm", o] + 1)
            for c in range(2):
                nc.vector.tensor_scalar(r_norm[:, c * CH:(c + 1) * CH], side[c][:], EPS, None, ALU.add).then_inc(side_free[c], 1)
            dve.drain()
            nc.vector.reciprocal(r_norm[:], r_norm[:])
            dve.drain()
            for c in range(2):
                ch = slice(c * CH, (c + 1) * CH)
                dve.wait_ge(filt_s, 6 * o + 4 + c + 1)
                for m in range(2):
                    for ft in range(TT):
                        a = nc.vector.tensor_tensor(K[o][m][:, ft, ch], acc[m][ft][:], r_norm[:, ch], ALU.mult)
                    a.then_inc(acc_free[m], 1)
        dve.drain()

        dve.wait_ge(idft_in, 32)
        for o in range(2):
            for c in range(2):
                ch = slice(c * CH, (c + 1) * CH)
                dve.wait_ge(filt_s, 12 + 2 * o + c + 1)
                for m, (zi, zj) in enumerate(((0, 1), (1, 0))):
                    for ft in range(TT):
                        nc.vector.tensor_tensor(Yf[c][m][:, ft], acc[zi][ft][:], K[o][0][:, ft, ch], ALU.mult)
                        a = nc.vector.tensor_tensor(Yt[ft][:], acc[zj][ft][:], K[o][1][:, ft, ch], ALU.mult)
                        if (m, ft) == (1, 1):
                            a.then_inc(acc_free[0], 1)
                            dve.sem_inc(acc_free[1], 1)
                    dve.drain()
                    for ft in range(TT):
                        a = nc.vector.tensor_tensor(Yf[c][m][:, ft], Yf[c][m][:, ft], Yt[ft][:], (ALU.add, ALU.subtract)[m])
                    if m == 1:
                        a.then_inc(yf_s, 1)
                    dve.drain()
            for c in range(2):
                ch = slice(c * CH, (c + 1) * CH)
                dve.drain()
                nc.vector.tensor_tensor(hy_t[:], hy[0][:, :, ch], hy_b[:, o, ch].unsqueeze(1).to_broadcast([P, TT, CH]), ALU.mult)
                dve.drain()
                for i in range(TT):
                    dve.wait_ge(side_full[i], SIDE[i]["conv", o, c] + 1)
                    nc.vector.tensor_tensor(hy_t[:, i], hy_t[:, i], side[i][:], ALU.add).then_inc(side_free[i], 1)
                dve.drain()
                nc.vector.tensor_tensor(hy[0][:, :, ch], hy_t[:], hy[1 + o][:, :, ch], ALU.mult).then_inc(conv_s, 1)
                dve.drain()
        nc.vector.tensor_tensor(hy_sq[:], hy[0][:], hy[0][:], ALU.mult)
        dve.drain()
        nc.vector.tensor_reduce(ss2[:, 1], hy_sq[:].rearrange("p t (g w) -> p (t g) w", w=P), X_AXIS, ALU.add)
        dve.drain()
        nc.vector.tensor_scalar(ss2[:, 1], ss2[:, 1], 1.0 / P, EPS, ALU.mult, ALU.add).then_inc(stat, 1)
        def mix_low(m):
            name, kt0, col = (("ssd", 8, V_SSD), ("hy", 0, V_HY))[m]
            for i in range(4):
                b, _ = UNITS[name, i]
                dve.wait_ge(part2_hi, 16 + 4 * m + i + 1)
                for f in range(2):
                    kt = 2 * i + f
                    a = nc.vector.scalar_tensor_tensor(in_l[:, kt0 + kt], tb[b][:, f * TOK:(f + 1) * TOK], table2[:, col + kt:col + kt + 1],
                                                       in_h[:, kt0 + kt].bitcast(F32), ALU.mult, ALU.subtract)
                a.then_inc(t_free[b], 1)

        mix_low(0)
        dve.wait_ge(rstd, 18)
        z_groups = hy[0][:].rearrange("p t (g w) -> p (t g) w", w=P)
        nc.vector.tensor_tensor(z_groups, z_groups, rstd2[:, 1].unsqueeze(2).to_broadcast([P, 16, P]), ALU.mult).then_inc(mix_s, 1)
        for n in (2, 3):
            split_lo2(OUT0 + n)
        mix_low(1)

        def gated_add(g, p, c):
            ch = slice(c * CH, (c + 1) * CH)
            for i in range(TT):
                a = nc.vector.tensor_tensor(res_t[p][:, i], acc[p][i][:], g_rows[g][:, ch], ALU.mult)
            a.then_inc(acc_free[p], 1)
            dve.drain()
            nc.vector.tensor_tensor(x_sb[:, :, ch], x_sb[:, :, ch], res_t[p][:], ALU.add).then_inc(x_up, 1)

        for n in range(16):
            if n >= 2:
                split_lo2(OUT0 + n + 2)
            if n in OUT_LAST:
                sl, r = ring(OUT0 + n)
                dve.wait_ge(w_free[sl], r + 1)
                c = OUT_LAST.index(n)
                gated_add(0, c % 2, c)
        x_norm(56, 19)
        diagonal(0, x_rstd)
        whole([("n2", i) for i in range(8)], in_f, in_l, in_h, 2, lambda kt: mod[:, 48 + kt, 0:1], 24)

        def hidden(q, last):
            hq = 8 * q if last else dve.snap(q * 8)
            aq = 4 * q if last else dve.snap(q * 4)
            for n in range(32):
                if not (last and n >= 30):
                    s = (MLP0 + n + 2) % NS
                    r = ring(MLP0 + n + 2, q)[1]
                    dve.wait_ge(w_hi[s], r)
                    nc.vector.tensor_tensor(lo[s][:], raw[s][:], hi[s][:].bitcast(F32), ALU.subtract).then_inc(w_lo[s], 1)
                if n % NS == 1 and 1 <= n // NS <= 4:
                    c = n // NS - 1
                    for u in range(2):
                        dve.wait_ge(hid_hi, hq + (2 * c + u + 1))
                        two = slice(4 * c + 2 * u, 4 * c + 2 * u + 2)
                        nc.vector.tensor_tensor(hid_l[:, two].rearrange("p k n -> p (k n)"), tb[u][:],
                                                hid_h[:, two].rearrange("p k n -> p (k n)").bitcast(F32), ALU.subtract).then_inc(t_free[u], 1)
                if n % NS == 3:
                    c, p = n // NS % 4, n // NS % 2
                    if n >= 16:
                        dve.wait_ge(w_free[(MLP0 + n) % NS], ring(MLP0 + n, q)[1] + 1)
                        gated_add(1, p, c)
                    else:
                        dve.wait_ge(acc_free[p], aq + (MLP_A[p] + c // 2 + 1))
                        nc.vector.tensor_tensor(y2[p][:], y2[p][:], y2[p][:], ALU.mult).then_inc(hid_sq, 1)

        with dve.Fori(0, 3) as q:
            hidden(q, False)
        hidden(3, True)
        x_norm(64, 20)
        dve.wait_ge(fnorm_in, 16)
        for i in range(TT):
            for c in range(4):
                ch = slice(c * CH, (c + 1) * CH)
                nc.vector.scalar_tensor_tensor(x_sb[:, i, ch], x_sb[:, i, ch], x_rstd[:, i:i + 1], f_norm[:, ch], ALU.mult, ALU.mult).then_inc(final_s, 1)

    @block.tensor
    def _(pe):
        def product(p, s, r, ah_, al_, k0, n, ktn):
            pe.wait_ge(w_lo[s], r)
            for k in range(n):
                kt = k0 + k
                for i in range(TT):
                    tok = slice(i * P, (i + 1) * P)
                    nc.tensor.matmul(acc[p][i][:], ah_[:, kt, tok], hi[s][:, k], start=(kt == 0), stop=False)
                    nc.tensor.matmul(acc[p][i][:], ah_[:, kt, tok], lo[s][:, k], start=False, stop=False)
                    last = nc.tensor.matmul(acc[p][i][:], al_[:, kt, tok], hi[s][:, k], start=False, stop=(kt == ktn - 1))
            last.then_inc(w_free[s], 1)

        def ada_total(i):
            pe.wait_ge(ada_mod, i + 1)
            pe.wait_ge(a_used, i * ADA_PIECES + (ADA_PIECES + 2))
            pe.wait_ge(term_used, i * KT + (KT + 2))
            for f in range(4):
                for c in range(2):
                    last = nc.tensor.matmul(side[0][:, 2 * f + c:2 * f + c + 1], ada_sum[c][:, f * P:(f + 1) * P], one[:], start=True, stop=True)
            last.then_inc(ada_post, 1)

        def turn(l, u, blocks):
            b, k = unit(l, u)
            pe.wait_ge(t_free[b], k)
            for i, src in enumerate(blocks):
                last = nc.tensor.transpose(tb[b][:, i * P:(i + 1) * P], src, ident[:])
            last.then_inc(t_full[b], 1)

        def turn_features(l, u0, src, n):
            for i in range(n // 2):
                turn(l, u0 + i, [src[:, j, kt * P:(kt + 1) * P] for kt in (2 * i, 2 * i + 1) for j in range(TT)])

        def turn_normed1(l, u0):
            for u in range(KT // 2):
                b, k = unit(l, u0 + u)
                pe.wait_ge(t_free[b], k)
                for i in range(4):
                    kt, j = 2 * u + i // 2, i % 2
                    last = nc.tensor.matmul(tb[b][:, i * P:(i + 1) * P], x_sb[:, j, kt * P:(kt + 1) * P], x_diag[:, j], start=True, stop=True)
                last.then_inc(t_full[b], 1)

        pe.wait_ge(consts, 64)
        pe.wait_ge(staged_in, 48)
        for b in range(2):
            nc.tensor.transpose(tb[b][:, 0:P], staged[:, b], ident[:]).then_inc(t_full[b], 1)
        pe.wait_ge(ctx_tick, 1)

        with pe.Fori(0, 2) as l:
            pe.wait_ge(staged_in, l * 144 + 192)
            turn(l, U_TAB, [staged[:, j] for j in range(2)])
            turn(l, U_TAB + 1, [staged[:, j] for j in range(2, 5)])
            pe.wait_ge(xn_ready, l * 4 + 2)
            turn_normed1(l, U_N1)

            def inputs_ready(u_end):
                for u in (u_end - 2, u_end - 1):
                    b, k = unit(l, u)
                    pe.wait_ge(t_free[b], k + 1)

            def head_scores(g, i):
                for u in range(2):
                    b, k = unit(l, (U_SA, U_SB)[g] + 2 * i + u)
                    pe.wait_ge(t_free[b], k)
                    for h in range(2):
                        last = nc.tensor.matmul(tb[b][:, h * TOK:(h + 1) * TOK], qkT[:, 4 * g + 2 * u + h, i * P:(i + 1) * P],
                                                qkT[:, 8 + g], start=True, stop=True)
                    last.then_inc(t_full[b], 1)

            def turn_probs(g, i):
                for u in range(2):
                    turn(l, (U_PA, U_PB)[g] + 2 * i + u,
                         [scores[g][:, i, 2 * u + h, kb * P:(kb + 1) * P] for h in range(2) for kb in range(TT)])

            def values(g, i):
                b, k = unit(l, (U_VA, U_VB)[g] + i)
                pe.wait_ge(t_free[b], k)
                for h in range(4):
                    for kb in range(TT):
                        last = nc.tensor.matmul(tb[b][:, h * HD:(h + 1) * HD], pT[:, i, h, kb],
                                                v_sb[:, kb, g * HD:(g + 1) * HD], start=(kb == 0), stop=(kb == 1))
                last.then_inc(t_full[b], 1)

            def spatial(i):
                for u in range(2):
                    b, k = unit(l, U_F + 2 * i + u)
                    pe.wait_ge(t_free[b], k)
                    for h in range(4 * u, 4 * u + 4):
                        last = nc.tensor.matmul(tb[b][:, (h % 4) * HD:(h % 4 + 1) * HD], wsT[:, h], gv[:, i, h * HD:(h + 1) * HD], start=True, stop=True)
                    last.then_inc(t_full[b], 1)

            def banks_read(g_units):
                for u in g_units:
                    b, k = unit(l, u)
                    pe.wait_ge(t_free[b], k + 1)

            inputs_ready(U_N1 + 8)
            reads = [1, 1]
            for c in range(7):
                p = c % 2
                r = pe.snap(rnd(l, R_IN + c))
                pe.wait_ge(acc_free[p], l * AL[p] + reads[p])
                reads[p] += 4 if c == 1 else 2
                for s in range(NS):
                    product(p, s, r, in_h, in_l, 4 * s, 4, KT)
                    if (c, s) == (1, 0):
                        pe.wait_ge(params, l * 96 + 96)
                        for i in range(2):
                            turn(l, U_WS + i, [ws_raw[:, h] for h in range(4 * i, 4 * i + 4)])
                    if (c, s) == (3, 1):
                        pe.wait_ge(roped_s, l * 3 + 1)
                        for i in range(TT):
                            turn(l, U_QKA + i, [roped[:, i, h] for h in range(4)])
                    if (c, s) == (3, 2):
                        pe.wait_ge(roped_s, l * 3 + 2)
                        for i in range(TT):
                            turn(l, U_QKA + 2 + i, [roped[:, i, h] for h in (8, 9)])
                    if (c, s) == (4, 0):
                        pe.wait_ge(roped_s, l * 3 + 3)
                        for i in range(TT):
                            turn(l, U_QKB + i, [roped[:, i, h] for h in range(4, 8)])
                    if c == 4 and s in (1, 2):
                        if s == 1:
                            banks_read((U_QKB, U_QKB + 1))
                        head_scores(0, s - 1)
                    if c == 5 and s < 2:
                        head_scores(1, s)
                    if c == 5 and s >= 2:
                        if s == 2:
                            pe.wait_ge(expd, l * 2 + 1)
                        turn_probs(0, s - 2)
                    if (c, s) == (6, 0):
                        banks_read((U_PA + 2, U_PA + 3))
                        values(0, 0)
                        values(0, 1)
                    if c == 6 and s in (1, 2):
                        if s == 1:
                            pe.wait_ge(vn_s, l + 1)
                        spatial(s - 1)
                    if (c, s) == (6, 3):
                        pe.wait_ge(expd, l * 2 + 2)
                        turn_probs(1, 0)
                        turn_probs(1, 1)
            banks_read((U_PB + 2, U_PB + 3))
            values(1, 0)
            values(1, 1)
            pe.wait_ge(half_s, l * 4 + 2)
            turn_features(l, U_AT, attn, 8)
            pe.wait_ge(half_s, l * 4 + 4)
            turn_features(l, U_GT, gated, 8)
            with pe.Fori(0, 2) as cp:
                for q in range(2):
                    r = pe.snap(rnd(l, R_O + q) + cp * 2)
                    if q == 0:
                        inputs_ready(U_GT + 4)
                    pe.wait_ge(acc_free[q], l * AL[q] + cp * 2 + reads[q])
                    for s in range(NS):
                        product(q, s, r, in_h, in_l, 4 * s, 4, KT)
            reads[0] += 4
            reads[1] += 4
            pe.wait_ge(xn_ready, l * 4 + 4)
            turn_normed1(l, U_N2)

            def turn_chunk(j, c):
                pe.wait_ge(acc_free[c], l * AL[c] + j * 2 + (reads[c] + 2))
                for u in range(2):
                    pe.wait_ge(t_free[u], l * (UL // 2) + j * 2 + (U_UP // 2 + 2 + c))
                    for f in range(2 * u, 2 * u + 2):
                        for i in range(TT):
                            at = (f % 2) * TOK + i * P
                            last = nc.tensor.transpose(tb[u][:, at:at + P], y[c][:, i, f * P:(f + 1) * P], ident[:])
                    last.then_inc(t_full[u], 1)

            def up_pair(j, before):
                r = pe.snap(rnd(l, R_UP) + j * 2)
                pe.wait_ge(acc_free[0], l * AL[0] + j * 2 + reads[0])
                for s in range(NS):
                    product(0, s, r, in_h, in_l, 4 * s, 4, KT)
                    if s == 0 and before is not None:
                        turn_chunk(before, 1)
                        ada_total(l * NPAIR + before)
                pe.wait_ge(acc_free[1], l * AL[1] + j * 2 + reads[1])
                for s in range(NS):
                    product(1, s, r + 1, in_h, in_l, 4 * s, 4, KT)
                    if s == 0:
                        turn_chunk(j, 0)

            inputs_ready(U_UP)
            up_pair(0, None)
            with pe.Fori(1, NPAIR) as j:
                up_pair(j, pe.snap(j + (-1)))
            pe.wait_ge(acc_free[0], l * AL[0] + reads[0] + 2 * NPAIR)
            for i in range(12):
                pe.wait_ge(al_s, l * 12 + i + 1)
                product(0, i % NS, rnd(l, R_DN + i // NS), ah, al, DN_AT[i], DN_SIZES[i], FT)
                if i == 0:
                    turn_chunk(NPAIR - 1, 1)
                    ada_total(l * NPAIR + (NPAIR - 1))
            reads[0] += 2 * NPAIR
            reads[1] += 2 * NPAIR
            with pe.Fori(1, 4) as c:
                r = pe.snap(rnd(l, R_DN) + c * 3)
                pe.wait_ge(acc_free[1], l * AL[1] + c * 2 + (reads[1] - 2))
                for i in range(12):
                    product(1, i % NS, r + i // NS, ah, al, DN_AT[i], DN_SIZES[i], FT)

        def product2(n, k0, streams, q=0, first=0, final=KT - 1):
            s, r = ring(n, q)
            pe.wait_ge(w_lo[s], r)
            dt = n == FIRST[DT]
            wh, wl = (dt_view(hi[s]), dt_view(lo[s])) if dt else (hi[s], lo[s])
            for p, h_, l_, cols in streams:
                for k in range(KT if dt else 4):
                    kt = k0 + k
                    for i in range(TT):
                        tok = slice(i * P, (i + 1) * P)
                        o = acc[p][i][:, 0:cols]
                        nc.tensor.matmul(o, h_[:, kt, tok], wh[:, k, 0:cols], start=(kt == first), stop=False)
                        nc.tensor.matmul(o, h_[:, kt, tok], wl[:, k, 0:cols], start=False, stop=False)
                        last = nc.tensor.matmul(o, l_[:, kt, tok], wh[:, k, 0:cols], start=False, stop=(kt == final))
            last.then_inc(w_free[s], 1)

        def take(use):
            p, k = USES[use]
            pe.wait_ge(acc_free[p], k)
            return p

        def read(use):
            p, k = USES[use]
            pe.wait_ge(acc_free[p], k + 1)

        def fill(u):
            b, k = UNITS[u]
            pe.wait_ge(t_free[b], k)
            return b

        def emptied(u):
            b, k = UNITS[u]
            pe.wait_ge(t_free[b], k + 1)

        def fill_side(b, use):
            k = SIDE[b][use]
            if k > 0:
                pe.wait_ge(side_free[b], k)
            return side[b]

        def turn2(u, blocks, to=None):
            b = fill(u)
            for i, src in enumerate(blocks):
                if to is None:
                    last = nc.tensor.transpose(tb[b][:, i * P:(i + 1) * P], src, ident[:])
                else:
                    last = nc.tensor.matmul(tb[b][:, i * P:(i + 1) * P], src, to[i % TT], start=True, stop=True)
            last.then_inc(t_full[b], 1)

        def turn_normed(name, src, which):
            for i in range(8):
                turn2((name, i), [src[:, j, kt * P:(kt + 1) * P] for kt in (2 * i, 2 * i + 1) for j in range(TT)],
                      [diag[:, which, j] for j in range(TT)])

        def forward(n, s):
            read(("in", n, s))
            y_ = conv_buffers(n, s)[0]
            for u in range(tiles_of((n, s)) // 2):
                turn2(("F", n, s, u), [y_[:, i, f * P:(f + 1) * P] for f in (2 * u, 2 * u + 1) for i in range(TT)])

        def backward(n, s):
            cv_ = conv_buffers(n, s)[1]
            for u in range(tiles_of((n, s)) // 2):
                emptied(("F", n, s, u))
            if (n, s) == (2, "c"):
                turn2(("B", n, s, 0), [cv_[:, f, i * P:(i + 1) * P] for i in range(TT) for f in range(2)])
            else:
                for i in range(TT):
                    turn2(("B", n, s, i), [cv_[:, f, i * P:(i + 1) * P] for f in range(4)])

        LE, GT, ONES, LT, GE = range(5)

        def running_sums():
            o = fill_side(0, "cum")
            pe.wait_ge(da_s, 1)
            for m in range(2):
                near = ((LE, GE), (GT, LT))[m]
                for i in range(TT):
                    for d in range(2):
                        at_ = 64 * m + 32 * i + NH * d
                        other = (i == 1) == ((m == 0) == (d == 0))
                        col = lambda k: dt_da[:, 2 * m + k, d * NH:(d + 1) * NH]
                        last = nc.tensor.matmul(o[:, at_:at_ + NH], masks[:, near[d]], col(i), start=True, stop=not other)
                        if other:
                            last = nc.tensor.matmul(o[:, at_:at_ + NH], masks[:, ONES], col(1 - i), start=False, stop=True)
            last.then_inc(side_full[0], 1)

        def end_states(d):
            pe.wait_ge(xw_s, d + 1)
            for g in range(2):
                o = fill_side(g, ("state", d))
                for i in range(TT):
                    last = nc.tensor.matmul(o[:], b_ctx[:, i, g * P:(g + 1) * P], xw[d][:, i, g * CH:(g + 1) * CH], start=(i == 0), stop=(i == 1))
                last.then_inc(side_full[g], 1)

        def last_total(i):
            sl, r = ring(max(n for n in ADA2 if ADA2[n][0] == i))
            o = fill_side(0, ("ada", i))
            pe.wait_ge(w_free[sl], r + 1)
            for f in range(4):
                last = nc.tensor.matmul(o[:, f:f + 1], ada_last[i - 22][:, f * P:(f + 1) * P], one[:], start=True, stop=True)
            last.then_inc(side_full[0], 1)

        pe.wait_ge(staged2, 16 * 12)
        turn2("tab", [staged[:, 0]])
        turn2("tab2", [staged[:, 1]])
        pe.wait_ge(ctx_in, 16)
        pe.wait_ge(diag_s, 1)
        turn_normed("ctx", ctx_sb, 1)
        pe.wait_ge(diag_s, 2)
        turn_normed("x", x_sb, 0)
        pe.wait_ge(ada_mod, 23)
        pe.wait_ge(part2_lo, 16)
        for j in range(12):
            cols = CHUNKS[j][2]
            streams = [(take(("in", j, "x")), in_h, in_l, 32 if j == DT else CH)]
            if j < SHARED:
                streams.append((take(("in", j, "c")), hc_h, hc_l, cols))
            for n, s in pieces_of(j):
                if s is None:
                    continue
                product2(n, 4 * s, streams)
                if (j, s) == (SHARED + 4, 1):
                    last_total(22)
                if j in (1, 2):
                    (forward, backward)[s // 2](j - 1, "xc"[s % 2])
                if j == SHARED and s < 2:
                    forward(2, "xc"[s])
                if (j, s) == (SHARED, 3):
                    backward(2, "c")
                if SHARED < j <= SHARED + 6 and s % 2 == 0:
                    (forward, backward)[s // 2](j - 1, "x")
                if (j, s) == (SHARED + 1, 1):
                    running_sums()
                if j == SHARED + 2 and s % 2 == 1:
                    end_states(s // 2)
                if j == SHARED + 3 and s % 2 == 1:
                    b = fill(f"f{s // 2 + 1}")
                    if s == 1:
                        pe.wait_ge(filt_in, 16 * 8)
                        last = nc.tensor.matmul(tb[b][0:HY_HID, 0:TOK], fw1[:], feats[:], start=True, stop=True)
                    else:
                        pe.wait_ge(sin_s, 1)
                        last = nc.tensor.matmul(tb[b][0:HY_HID, 0:TOK], fw2[:], hdn[0][:], start=True, stop=True)
                    last.then_inc(t_full[b], 1)

        last_total(23)
        pe.wait_ge(bc_s, 1)
        for g in range(2):
            o = fill_side(g, "CB")
            for i in range(TT):
                last = nc.tensor.matmul(o[:, i * TOK:(i + 1) * TOK], bcT[:, g, i * P:(i + 1) * P], bcT[:, 2 + g], start=True, stop=True)
            last.then_inc(side_full[g], 1)

        def head_sums(h, m):
            pe.wait_ge(dlh_s, h + 1)
            for d in range(2):
                b, k = UNITS["E", 0, d]
                pe.wait_ge(t_free[b], h + k)
                near, w = (LE, GE)[d], dlh[m]
                own = ((0, 0), (2 * P, P)) if d == 0 else ((P, 0), (2 * P, 2 * P))
                across = P if d == 0 else 0
                for at_, l0 in own:
                    nc.tensor.matmul(tb[b][:, at_:at_ + P], w[:, d, l0:l0 + P], masks[:, near], start=True, stop=True)
                part = 2 * P if d == 0 else P
                nc.tensor.matmul(tb[b][:, across:across + P], w[:, d, 0:P], masks[:, ONES], start=True, stop=False)
                last = nc.tensor.matmul(tb[b][:, across:across + P], w[:, d, part:part + P], masks[:, near], start=False, stop=True)
                last.then_inc(t_full[b], 1)

        def head_outputs(h, g, m, at_):
            pe.wait_ge(mt_s, h + 1)
            blk = lambda d, n: decays[m][:, d, n * P:(n + 1) * P]
            val = lambda d, i: xdt[d][:, i, ds(at_ + g * CH, PH)]
            for i, terms in enumerate((((0, 0, 0), (1, 0, 1), (1, 2, 0)), ((0, 1, 0), (0, 2, 1), (1, 1, 1)))):
                for n, (d, blk_n, src) in enumerate(terms):
                    last = nc.tensor.matmul(acc[g][i][:, ds(at_, PH)], blk(d, blk_n), val(d, src), start=(n == 0), stop=(n == 2))
            last.then_inc(mt_used, 1)

        head_sums(0, 0)
        for g in range(2):
            take(("y", g))
            with pe.Fori(0, 4 - g) as hp:
                head_sums(pe.snap(hp * 2 + (8 * g + 1)), 1)
                head_outputs(pe.snap(hp * 2 + 8 * g), g, 0, pe.snap(hp * (2 * PH)))
                head_sums(pe.snap(hp * 2 + (8 * g + 2)), 0)
                head_outputs(pe.snap(hp * 2 + (8 * g + 1)), g, 1, pe.snap(hp * (2 * PH) + PH))
            if g == 1:
                head_sums(NH - 1, 1)
                head_outputs(NH - 2, g, 0, 6 * PH)
                head_outputs(NH - 1, g, 1, 7 * PH)
            nc.tensor.sem_inc(y_done, 1)
        for g in range(2):
            for i in range(TT):
                for d in range(2):
                    o = fill_side(d, ("off", g, i))
                    nc.tensor.matmul(o[:], bcT[:, 2 + g, i * P:(i + 1) * P], states[:, d, g * CH:(g + 1) * CH], start=True, stop=True).then_inc(side_full[d], 1)

        pe.wait_ge(sin_s, 2)
        pe.wait_ge(fw3_in, 32)
        for o in range(2):
            for i in range(4):
                p = take(("h", o, i))
                for tt in range(TT):
                    last = nc.tensor.matmul(acc[p][tt][:], hdn[1][:, tt * P:(tt + 1) * P], fw3[o][:, i * CH:(i + 1) * CH], start=True, stop=True)
                last.then_inc(filt_s, 1)
            for d in range(2):
                for c in range(2):
                    ps_ = fill_side(c, ("norm", o))
                    pe.wait_ge(abs_s, 4 * o + 2 * d + c + 1)
                    for tt in range(TT):
                        last = nc.tensor.matmul(ps_[:], masks[:, ONES], h_abs[d][:, tt, c * CH:(c + 1) * CH], start=(d + tt == 0), stop=(d + tt == 2))
                    if d == 1:
                        last.then_inc(side_full[c], 1)
            pe.wait_ge(filtered, o + 1)
            for c in range(2):
                for m, src in enumerate((h_sum, h_1)):
                    p = take(("K", o, c, m))
                    for ft in range(TT):
                        for tt in range(TT):
                            last = nc.tensor.matmul(acc[m][ft][:], dft[:, m, tt, ft * P:(ft + 1) * P], src[:, tt, c * CH:(c + 1) * CH], start=(tt == 0), stop=(tt == 1))
                last.then_inc(filt_s, 1)
        def spread_gate(i):
            b = fill(("g", i))
            pe.wait_ge(gdiag_s, i + 1)
            for f in range(4):
                last = nc.tensor.matmul(tb[b][:, f * P:(f + 1) * P], masks[:, ONES], g_diag[:, f], start=True, stop=True)
            last.then_inc(t_full[b], 1)

        pe.wait_ge(idft_in, 32)
        for o in range(2):
            for c in range(2):
                if o > 0:
                    pe.wait_ge(conv_s, c + 1)
                for m in range(2):
                    take(("Z", o, c, m))
                    for ft in range(TT):
                        for tt in range(TT):
                            last = nc.tensor.matmul(acc[m][ft][:], dft[:, m, tt, ft * P:(ft + 1) * P], hy[0][:, tt, c * CH:(c + 1) * CH], start=(tt == 0), stop=(tt == 1))
                last.then_inc(filt_s, 1)
                spread_gate(4 * o + 2 * c)
                spread_gate(4 * o + 2 * c + 1)
            for c in range(2):
                pe.wait_ge(yf_s, 2 * o + c + 1)
                for i in range(TT):
                    o_ = fill_side(i, ("conv", o, c))
                    for m in range(2):
                        for ft in range(TT):
                            last = nc.tensor.matmul(o_[:], idft[:, m, ft, i * P:(i + 1) * P], Yf[c][m][:, ft], start=(m + ft == 0), stop=(m + ft == 2))
                    last.then_inc(side_full[i], 1)
        def turn_branch(m):
            name, src = (("ssd", xs[0]), ("hy", hy[0]))[m]
            pe.wait_ge(mix_s, m + 1)
            for i in range(4):
                turn2((name, i), [src[:, j, kt * P:(kt + 1) * P] for kt in (2 * i, 2 * i + 1) for j in range(TT)])

        turn_branch(0)
        for n, (c, k) in enumerate(OUT):
            if k == 2 and n < NS:
                for i in (2, 3):
                    emptied(("ssd", i))
            if n == NS:
                turn_branch(1)
                for i in (2, 3):
                    emptied(("hy", i))
            if n in OUT_FIRST:
                p = take(("out", c))
            product2(OUT0 + n, 4 * k, [(c % 2, in_h, in_l, CH)], 0, 4 * OUT[OUT_FIRST[c]][1], 4 * OUT[OUT_LAST[c]][1] + 3)
        pe.wait_ge(diag_s, 3)
        turn_normed("n2", x_sb, 0)
        pe.wait_ge(part2_lo, 24)

        def hidden(q, last_q):
            aq = 4 * q if last_q else pe.snap(q * 4)

            def turn_hidden(c):
                p = c % 2
                pe.wait_ge(hid_sq, aq + (c + 1))
                for u in range(2):
                    pe.wait_ge(t_free[u], aq + (MLP_U + c))
                    for f in range(2 * u, 2 * u + 2):
                        for i in range(TT):
                            at_ = (f % 2) * TOK + i * P
                            last = nc.tensor.transpose(tb[u][:, at_:at_ + P], y2[p][:, i, f * P:(f + 1) * P], ident[:])
                    last.then_inc(t_full[u], 1)

            for c in range(4):
                p = c % 2
                pe.wait_ge(acc_free[p], aq + (MLP_A[p] + c // 2))
                for s in range(NS):
                    product2(MLP0 + NS * c + s, 4 * s, [(p, in_h, in_l, CH)], q)
                    if s == 0 and c > 0:
                        turn_hidden(c - 1)
            for c in range(4):
                p = c % 2
                pe.wait_ge(acc_free[p], aq + (MLP_A[p] + 2 + c // 2))
                for s in range(NS):
                    if c == 0:
                        for u in range(2):
                            pe.wait_ge(t_free[u], aq + (MLP_U + s + 1))
                    product2(MLP0 + 16 + NS * c + s, 4 * s, [(p, hid_h, hid_l, CH)], q)
                    if (c, s) == (0, 0):
                        turn_hidden(3)

        with pe.Fori(0, 3) as q:
            hidden(q, False)
        hidden(3, True)

    block_guard.__exit__(None, None, None)


def kernel(**inputs):
    import concourse.bacc as bacc
    from concourse import mybir
    from concourse.bass_utils import run_bass_kernel_spmd as run

    nc = bacc.Bacc("TRN2", target_bir_lowering=False, num_devices=1)
    arrays, aps = {}, {}
    for name, a in {**inputs, **shape_constants()}.items():
        a = np.ascontiguousarray(a)
        arrays[f"in_{name}"] = a
        aps[name] = nc.dram_tensor(f"in_{name}", a.shape, mybir.dt.from_np(a.dtype), kind="ExternalInput").ap()
    out = nc.dram_tensor("out_0", (1, TOK, D), mybir.dt.float32, kind="ExternalOutput").ap()
    program(nc, aps, out)
    r = run(nc, [arrays], core_ids=[0])
    return r.results[0]["out_0"]
```
